# Optimizing a Trainium2 kernel written in Bass

```python
import jax, jax.numpy as jnp
from jax import lax
import numpy as np

D_MODEL = 1024
BATCH = 1
SEQ = 256
DEPTH = 2

GRID_W = 64
N_FOURIER_GROUPS = 4
FOURIER_GROUP_DIM = D_MODEL // N_FOURIER_GROUPS
N_HEADS = 16
HEAD_DIM = D_MODEL // N_HEADS
WIN_H_MAX = 8
WIN_W = 16
D_FF_DENSE = 2816
N_EXPERTS = 8
TOP_K = 2
D_FF_EXPERT = 3584
MOE_BLOCK = 256
RMS_EPS = 1e-6
N_EVEN = (DEPTH + 1) // 2
N_ODD = DEPTH // 2

kernel_name = "hybrid_fnet_natten_moe_encoder"

def rms_norm(x, g):
    xf = x.astype(jnp.float32)
    y = xf * lax.rsqrt(jnp.mean(xf * xf, axis=-1, keepdims=True) + RMS_EPS)
    return (y * g.astype(jnp.float32)).astype(x.dtype)

def fourier_mixer(h, w_in, w_out):
    B, S, D = h.shape
    u = (h @ w_in).reshape(B, S, N_FOURIER_GROUPS, FOURIER_GROUP_DIM)
    f = jnp.fft.fft2(u.astype(jnp.float32), axes=(1, 3), norm="ortho").real
    return f.astype(h.dtype).reshape(B, S, D) @ w_out

def neighbourhood_attention(h, w_qkv, rpb, w_o):
    B, S, D = h.shape
    rows = S // GRID_W
    kh = min(WIN_H_MAX, rows)
    qkv = (h @ w_qkv).reshape(B, rows, GRID_W, 3, N_HEADS, HEAD_DIM)
    q = qkv[:, :, :, 0] * (HEAD_DIM ** -0.5)
    k = qkv[:, :, :, 1]
    v = qkv[:, :, :, 2]
    r = jnp.arange(rows)
    row_start = jnp.clip(r - kh // 2, 0, rows - kh)
    c = jnp.arange(GRID_W)
    col_start = jnp.clip(c - WIN_W // 2, 0, GRID_W - WIN_W)
    col_idx = col_start[:, None] + jnp.arange(WIN_W)[None, :]
    dr = row_start[:, None] + jnp.arange(kh)[None, :] - r[:, None] + (WIN_H_MAX - 1)
    dc = col_idx - c[:, None] + (WIN_W - 1)
    bias = rpb[:, dr[:, None, :, None], dc[None, :, None, :]]
    bias = jnp.moveaxis(bias, 1, 0).astype(jnp.float32)

    def row_block(args):
        q_r, s, b_r = args
        k_rows = lax.dynamic_slice_in_dim(k, s, kh, axis=1)
        v_rows = lax.dynamic_slice_in_dim(v, s, kh, axis=1)
        k_g = k_rows[:, :, col_idx]
        v_g = v_rows[:, :, col_idx]
        sc = jnp.einsum('bwhd,bawkhd->bhwak', q_r, k_g).astype(jnp.float32) + b_r[None]
        p = jax.nn.softmax(sc.reshape(B, N_HEADS, GRID_W, kh * WIN_W), axis=-1)
        p = p.reshape(sc.shape).astype(v.dtype)
        return jnp.einsum('bhwak,bawkhd->bwhd', p, v_g)

    out = lax.map(row_block, (jnp.moveaxis(q, 1, 0), row_start, bias))
    out = jnp.moveaxis(out, 0, 1).reshape(B, S, D)
    return out @ w_o

def swiglu(h, w_gate, w_up, w_down):
    return (jax.nn.silu(h @ w_gate) * (h @ w_up)) @ w_down

def moe_swiglu(h, w_router, b_router, w_gate, w_up, w_down):
    B, S, D = h.shape
    t = h.reshape(-1, D)
    T = t.shape[0]
    TK = T * TOP_K
    logits = (t @ w_router).astype(jnp.float32) + b_router.astype(jnp.float32)
    top_val, top_idx = lax.top_k(logits, TOP_K)
    gates = jax.nn.softmax(top_val, axis=-1)
    flat_e = top_idx.reshape(-1)
    flat_tok = jnp.arange(TK, dtype=jnp.int32) // TOP_K
    order = jnp.argsort(flat_e)
    e_sorted = flat_e[order]
    tok_sorted = flat_tok[order]
    g_sorted = gates.reshape(-1)[order]
    counts = jnp.bincount(flat_e, length=N_EXPERTS)
    padded = (counts + MOE_BLOCK - 1) // MOE_BLOCK * MOE_BLOCK
    start = jnp.cumsum(counts) - counts
    pend = jnp.cumsum(padded)
    pstart = pend - padded
    dest = pstart[e_sorted] + jnp.arange(TK) - start[e_sorted]
    n_blocks = -(-(TK + N_EXPERTS * (MOE_BLOCK - 1)) // MOE_BLOCK)
    row_tok = jnp.zeros((n_blocks * MOE_BLOCK,), jnp.int32).at[dest].set(tok_sorted)
    block_expert = jnp.minimum(
        jnp.searchsorted(pend, jnp.arange(n_blocks) * MOE_BLOCK, side='right'), N_EXPERTS - 1)
    xs = t[row_tok].reshape(n_blocks, MOE_BLOCK, D)

    def expert_block(args):
        xb, e = args
        return (jax.nn.silu(xb @ w_gate[e]) * (xb @ w_up[e])) @ w_down[e]

    ys = lax.map(expert_block, (xs, block_expert)).reshape(-1, D)
    y = ys[dest] * g_sorted[:, None].astype(h.dtype)
    out = jnp.zeros((T, D), h.dtype).at[tok_sorted].add(y)
    return out.reshape(B, S, D)

def setup_inputs(seed: int = 0) -> dict:
    key = jax.random.key(seed)
    ks = jax.random.split(key, 20)

    def w(k, shape, fan_in):
        return jax.random.normal(k, shape, jnp.float32) * (fan_in ** -0.5)

    return {
        "x": jax.random.normal(ks[0], (BATCH, SEQ, D_MODEL), jnp.float32),
        "norm_mix": 1.0 + 0.02 * jax.random.normal(ks[1], (DEPTH, D_MODEL), jnp.float32),
        "norm_ffn": 1.0 + 0.02 * jax.random.normal(ks[2], (DEPTH, D_MODEL), jnp.float32),
        "fourier_w_in": w(ks[3], (N_EVEN, D_MODEL, D_MODEL), D_MODEL),
        "fourier_w_out": w(ks[4], (N_EVEN, D_MODEL, D_MODEL), D_MODEL),
        "nat_w_qkv": w(ks[5], (N_ODD, D_MODEL, 3 * D_MODEL), D_MODEL),
        "nat_rpb": 0.1 * jax.random.normal(ks[6], (N_ODD, N_HEADS, 2 * WIN_H_MAX - 1, 2 * WIN_W - 1), jnp.float32),
        "nat_w_o": w(ks[7], (N_ODD, D_MODEL, D_MODEL), D_MODEL),
        "ffn_w_gate": w(ks[8], (N_EVEN, D_MODEL, D_FF_DENSE), D_MODEL),
        "ffn_w_up": w(ks[9], (N_EVEN, D_MODEL, D_FF_DENSE), D_MODEL),
        "ffn_w_down": w(ks[10], (N_EVEN, D_FF_DENSE, D_MODEL), D_FF_DENSE),
        "router_w": w(ks[11], (N_ODD, D_MODEL, N_EXPERTS), D_MODEL),
        "router_b": 0.01 * jax.random.normal(ks[12], (N_ODD, N_EXPERTS), jnp.float32),
        "expert_w_gate": w(ks[13], (N_ODD, N_EXPERTS, D_MODEL, D_FF_EXPERT), D_MODEL),
        "expert_w_up": w(ks[14], (N_ODD, N_EXPERTS, D_MODEL, D_FF_EXPERT), D_MODEL),
        "expert_w_down": w(ks[15], (N_ODD, N_EXPERTS, D_FF_EXPERT, D_MODEL), D_FF_EXPERT),
        "final_norm": 1.0 + 0.02 * jax.random.normal(ks[16], (D_MODEL,), jnp.float32),
    }

def reference(x, norm_mix, norm_ffn, fourier_w_in, fourier_w_out, nat_w_qkv, nat_rpb, nat_w_o,
              ffn_w_gate, ffn_w_up, ffn_w_down, router_w, router_b,
              expert_w_gate, expert_w_up, expert_w_down, final_norm):
    h = x
    for i in range(DEPTH):
        j = i // 2
        hn = rms_norm(h, norm_mix[i])
        if i % 2 == 0:
            mix = fourier_mixer(hn, fourier_w_in[j], fourier_w_out[j])
        else:
            mix = neighbourhood_attention(hn, nat_w_qkv[j], nat_rpb[j], nat_w_o[j])
        h = h + mix
        hn = rms_norm(h, norm_ffn[i])
        if i % 2 == 0:
            ff = swiglu(hn, ffn_w_gate[j], ffn_w_up[j], ffn_w_down[j])
        else:
            ff = moe_swiglu(hn, router_w[j], router_b[j], expert_w_gate[j], expert_w_up[j], expert_w_down[j])
        h = h + ff
    return rms_norm(h, final_norm)


_drawn_inputs = setup_inputs


def setup_inputs(seed=0):
    import zlib

    import numpy as np

    out = dict(_drawn_inputs(seed))
    spreads = {}
    factors = {'router_b': 4.34, 'final_norm': 2.865}
    for name, (base, spread) in spreads.items():
        noise = np.random.default_rng([zlib.crc32(name.encode()), seed]).standard_normal(out[name].shape)
        drawn = base * np.exp(spread * noise) if base else spread * noise
        out[name] = __import__('jax').numpy.asarray(drawn.astype(out[name].dtype))
    for name, factor in factors.items():
        out[name] = (out[name] * factor).astype(out[name].dtype)
    return out
```

```python
import concourse.bass as bass
from concourse import mybir
from contextlib import ExitStack
import numpy as np

P = 128
D = 1024
S = 256
NB = S // P
KD = D // P
GRID = 64
ROWS = S // GRID
WIN_W = 16
WIN_H_MAX = 8
HEADS = 16
HD = D // HEADS
GROUP = 256
FF = 2816
FFE = 3584
NE = 8
EPS = 1e-6
BANK = 512
PIECE = 2048
RAW = 6
SPLIT = 3
KH = PIECE // BANK
KROW = PIECE // D
RPB_H, RPB_W = 2 * WIN_H_MAX - 1, 2 * WIN_W - 1
SHIFTS = 2 * ROWS - 2
BIAS_W = 5
MASKED = -1e30


def dense_pieces(w_in, w_out, ffg, ffu, ffd, qkv, wo):
    def columns(w, c0, width=BANK):
        tiles = PIECE // width
        v = w.rearrange("(k p) n -> p k n", p=P)
        return [(v[:, k:k + tiles, c0:c0 + width], tiles, width) for k in range(0, KD, tiles)]

    def rows(w, r0, n_rows):
        v = w.rearrange("(k p) n -> p k n", p=P)
        return [(v[:, k:k + KROW, :], KROW, D) for k in range(r0 // P, (r0 + n_rows) // P, KROW)]

    out = {"w_in": [columns(w_in, c) for c in (0, BANK)], "w_out": [columns(w_out, c) for c in (0, BANK)],
           "qkv": [columns(qkv, c) for c in range(0, 3 * D, BANK)], "wo": [columns(wo, c) for c in (0, BANK)]}
    widths = [BANK] * (FF // BANK) + ([FF % BANK] if FF % BANK else [])
    out["gate"] = [columns(ffg, BANK * c, w) for c, w in enumerate(widths)]
    out["up"] = [columns(ffu, BANK * c, w) for c, w in enumerate(widths)]
    out["down"] = [rows(ffd, BANK * c, w) for c, w in enumerate(widths)]
    order = [x for k in ("w_in", "w_out") for x in out[k]]
    for c in range(len(widths)):
        order += [out["gate"][c], out["up"][c]]
        if c:
            order.append(out["down"][c - 1])
    order.append(out["down"][-1])
    order += out["qkv"] + out["wo"]
    flat = [piece for group in order for piece in group]
    where = {}
    n = 0
    for group in order:
        where[id(group)] = list(range(n, n + len(group)))
        n += len(group)
    index = {k: [where[id(g)] for g in v] for k, v in out.items()}
    return flat, index, widths


STEPS = FFE // BANK
def expert_pieces():
    order = []
    for c in range(STEPS):
        order += [("gate", c, 0), ("gate", c, 1), ("up", c, 0), ("up", c, 1)]
        if c:
            order += [("down", c - 1, 0), ("down", c - 1, 1)]
    order += [("down", STEPS - 1, 0), ("down", STEPS - 1, 1)]
    return order, {x: j for j, x in enumerate(order)}


EXPERT, AT = expert_pieces()
PER_EXPERT = len(EXPERT)
assert PER_EXPERT % RAW == 0 and PER_EXPERT % SPLIT == 0


def expert_source(ewg, ewu, ewd, e, j):
    kind, c, half = EXPERT[j]
    v = {"gate": ewg, "up": ewu, "down": ewd}[kind][0].rearrange("e (k p) n -> p (e k) n", p=P)
    if kind == "down":
        return v[:, bass.ds(e * (FFE // P) + (BANK // P * c + KROW * half), KROW), :], KROW, D
    return v[:, bass.ds(e * KD + KH * half, KH), BANK * c:BANK * (c + 1)], KH, BANK


def trunk(nc, x, norm_mix, norm_ffn, w_in, w_out, w_qkv, rpb, w_o, ffg, ffu, ffd, router_w, router_b,
          ewg, ewu, ewd, final_norm, dft_c, mask_c, band_c, ident_c, before_c, count_c, out):
    f32, f32r, i32 = mybir.dt.float32, mybir.dt.float32r, mybir.dt.int32
    ALU, ACT, AX = mybir.AluOpType, mybir.ActivationFunctionType, mybir.AxisListType

    dense, at, widths = dense_pieces(w_in[0], w_out[0], ffg[0], ffu[0], ffd[0], w_qkv[0], w_o[0])
    N0 = len(dense)
    dense += [expert_source(ewg, ewu, ewd, 0, j) for j in range(SPLIT)]
    N1 = len(dense)
    norm_gain = [norm_mix[0:1, :], norm_ffn[0:1, :], norm_mix[1:2, :], norm_ffn[1:2, :],
                 final_norm.rearrange("(a n) -> a n", a=1)]

    def sb(name, shape, dt=f32):
        return nc.alloc_sbuf_tensor(name, shape, dt)

    raw = [sb(f"raw{i}", [P, PIECE]) for i in range(RAW)]
    w_hi = [sb(f"w_hi{i}", [P, PIECE], f32r) for i in range(SPLIT)]
    w_lo = [sb(f"w_lo{i}", [P, PIECE], f32r) for i in range(SPLIT)]
    h = sb("h", [P, NB, D])
    hn = sb("hn", [P, NB, D])
    gain = sb("gain", [P, 2, D])
    act_hi = sb("act_hi", [P, KD, S], f32r)
    act_lo = sb("act_lo", [P, KD, S], f32r)
    ident = sb("ident", [P, P])
    sumsq = sb("sumsq", [P, 5, NB])
    rstd = sb("rstd", [P, 5, NB])
    half_power = sb("half_power", [P, NB])
    silu_g = [sb(f"silu_g{i}", [P, BANK]) for i in range(2)]
    hid = [sb(f"hid{i}", [P, BANK]) for i in range(2)]
    hidT_hi = [sb(f"hidT_hi{i}", [P, BANK], f32r) for i in range(2)]
    hidT_lo = [sb(f"hidT_lo{i}", [P, BANK], f32r) for i in range(2)]

    def width_of(shape):
        return -(-4 * int(np.prod(shape[1:])) // 32) * 32

    def layout(entries, off):
        made = {}
        for name, shape, dt in entries:
            made[name] = nc.alloc_sbuf_tensor_at(name, shape, dt, offset=off)
            off += width_of(shape)
        return made

    fourier_l = [("dft_hi", [P, NB, 3 * S], f32r), ("dft_lo", [P, NB, 3 * S], f32r),
                 ("u_hi", [P, NB, D], f32r), ("u_lo", [P, NB, D], f32r),
                 ("pt_hi", [P, KD, 2 * S], f32r), ("pt_lo", [P, KD, 2 * S], f32r)]
    attn_l = [("qk", [P, 2, NB, BANK], f32), ("qT", [P, KD, S], f32), ("kT", [P, KD, S], f32), ("v", [P, NB, D], f32),
              ("bias", [P, HEADS, SHIFTS, GRID], f32), ("mask", [P, GRID], f32),
              ("table", [2 * RPB_W, HEADS, SHIFTS], f32), ("band", [2 * RPB_W, P + GRID - 1], f32), ("probT", [P, 2, NB * S], f32),
              ("neg_max", [P, 2, NB], f32), ("p_sum", [P, 2, NB], f32), ("p_inv", [P, 2, NB], f32)]
    moe_l = [("hn_hi", [P, NB, D], f32r), ("hn_lo", [P, NB, D], f32r), ("xg_hi", [P, KD, P], f32r),
             ("xg_lo", [P, KD, P], f32r), ("y_hi", [P, D], f32r), ("y_lo", [P, D], f32r), ("sel", [P, NB, P], f32r),
             ("selT", [P, NB, P], f32r), ("rw", [P, KD, NE], f32), ("rw_hi", [P, KD, NE], f32r),
             ("rw_lo", [P, KD, NE], f32r), ("rb", [P, NE], f32), ("count", [P, S], f32), ("before", [P, P], f32),
             ("ones", [P, P], f32), ("logit", [P, NB, NE], f32), ("top", [P, 2, NB], f32), ("eq", [P, NB, NE], f32),
             ("cand", [P, NB, NE], f32), ("idx", [P, 2, NB], f32), ("first", [P, NB, NE], f32),
             ("second", [P, NB, NE], f32), ("rest", [P, NB, NE], f32), ("used", [P, NB, NE], f32),
             ("gap", [P, NB], f32), ("ratio", [P, NB], f32), ("den", [P, NB], f32), ("g1", [P, NB], f32),
             ("g2", [P, NB], f32), ("weight", [P, NB, NE], f32), ("slot", [P, NB, 2 * NE], f32),
             ("most", [P, 1], f32), ("flag", [P, 1], i32)]
    arena_start = -(-nc.sbuf_base // 32) * 32
    sizes = [sum(width_of(shape) for _, shape, _ in l) for l in (fourier_l, attn_l, moe_l)]
    sb("arena", [P, max(sizes) // 4])
    fo, att, mo = (layout(l, arena_start) for l in (fourier_l, attn_l, moe_l))
    fo |= layout([("dft_raw", [P, NB, 3 * S], f32)], arena_start + sum(width_of(shape) for _, shape, _ in fourier_l[:-1]))

    bank = {n: nc.alloc_psum_tensor(f"bank_{n}", [P, BANK], f32) for n in ("G0", "G1", "U0", "U1", "Y0", "Y1", "T0", "T1")}
    G, U, Y, T = ([bank[f"{n}0"], bank[f"{n}1"]] for n in "GUYT")

    TY = [T[0], T[1], Y[0], Y[1]]
    GU = [G[0], G[1], U[0], U[1]]

    def two(bk):
        return bk[:].rearrange("p (k s) -> p k s", k=2)

    def four(bk):
        return bk[:].rearrange("p (k s) -> p k s", k=4)

    def sem(name):
        return nc.alloc_semaphore(name)

    raw_in = [sem(f"raw_in{i}") for i in range(RAW)]
    hi_made, lo_made, piece_used = sem("hi_made"), sem("lo_made"), sem("piece_used")
    s_x, s_const, s_dft, s_mask, s_rout, s_out = (sem(f"s_{n}") for n in ("x", "const", "dft", "mask", "rout", "out"))
    s_gain = [sem("s_gain0"), sem("s_gain1")]
    h_ready, sq_done, rstd_chain, rstd_done, hn_done = (sem(n) for n in ("h_ready", "sq_done", "rstd_chain", "rstd_done", "hn_done"))
    tr_done, act_hi_done, act_lo_done = sem("tr_done"), sem("act_hi_done"), sem("act_lo_done")
    dft_hi_done, dft_lo_done, u_psum, u_hi_done, u_lo_done = (sem(n) for n in ("dft_hi_done", "dft_lo_done", "u_psum", "u_hi_done", "u_lo_done"))
    pt_psum, pt_hi_done, pt_lo_done, ft_psum, ft_hi_done, ft_lo_done, fo_psum = (sem(n) for n in (
        "pt_psum", "pt_hi_done", "pt_lo_done", "ft_psum", "ft_hi_done", "ft_lo_done", "fo_psum"))
    d_gate, d_silu, d_up, d_hid, d_hidT, d_hidT_hi, d_hidT_lo, d_down, d_added = (sem("d_" + n) for n in (
        "gate", "silu", "up", "hid", "hidT", "hidT_hi", "hidT_lo", "down", "added"))
    qkv_psum, qkv_act, qkv_dve, qkT_psum, qT_act, qT_dve = (sem(n) for n in (
        "qkv_psum", "qkv_act", "qkv_dve", "qkT_psum", "qT_act", "qT_dve"))
    bias_psum, bias_done, a_score, a_biased, a_max, a_exp, a_inv, a_norm, a_pT, a_pTcopy, a_pv, a_ohi, a_olo, ao_psum = (sem(n) for n in (
        "bias_psum", "bias_done", "a_score", "a_biased", "a_max", "a_exp", "a_inv", "a_norm", "a_pT", "a_pTcopy", "a_pv", "a_ohi", "a_olo", "ao_psum"))
    hnr_hi, hnr_lo, rw_hi_done, rw_lo_done, ones_done, logit_psum, gap_done, ratio_done, used_done, rank_psum, flag_done, dve_chain = (sem(n) for n in (
        "hnr_hi", "hnr_lo", "rw_hi_done", "rw_lo_done", "ones_done", "logit_psum", "gap_done", "ratio_done", "used_done", "rank_psum", "flag_done", "dve_chain"))
    e_silu, e_hid, e_hidT, e_hidT_hi, e_hidT_lo, e_selT, e_selT_copy, e_sel, e_gather, e_xhi, e_xlo, e_yhi, e_ylo, e_scatter, e_added = (
        sem("e_" + n) for n in ("silu", "hid", "hidT", "hidT_hi", "hidT_lo", "selT", "selT_copy",
                                "sel", "gather", "xhi", "xlo", "yhi", "ylo", "scatter", "added"))
    moe_done, fin_done = sem("moe_done"), sem("fin_done")

    NLAST = at["wo"][-1][-1]
    DC = len(widths)
    EXPERTS = {0: (0, NE), 1: (NE, 2 * NE)}

    def piece(j, E, back=0):
        return j + 1 - back if E is None else E * PER_EXPERT + (N0 + j + 1 - back)

    def slot_of(j, E, n):
        return (j if E is None else N0 + j) % n

    def has_before(j, E, back):
        return E is not None or j >= back

    def projected(eng, first_block, c, pieces, b):
        if b < NB - 1:
            eng.wait_ge(first_block, c + 1)
        else:
            eng.wait_ge(piece_used, pieces[-1] + 1)

    block = nc.Block()
    block.__enter__()

    @block.sync
    def _(sp):
        def load(j, E, src, tiles):
            s = slot_of(j, E, RAW)
            if has_before(j, E, RAW):
                sp.wait_ge(lo_made, piece(j, E, RAW))
            sp.dma_start(raw[s][:].rearrange("p (k n) -> p k n", k=tiles), src).then_inc(raw_in[s], 16)

        sp.dma_start(h[:], x[0].rearrange("(b p) d -> p b d", p=P)).then_inc(s_x, 16)
        for j, (src, tiles, _) in enumerate(dense):
            load(j, None, src, tiles)
            if j == 1:
                sp.dma_start(fo["dft_raw"][:], dft_c.rearrange("(b p) n -> p b n", p=P)).then_inc(s_dft, 16)

        def expert_loads(E):
            for j in range(SPLIT, PER_EXPERT + SPLIT):
                e = E % NE if j < PER_EXPERT else (E + 1) % NE
                src, tiles, _ = expert_source(ewg, ewu, ewd, e, j % PER_EXPERT)
                load(j, E, src, tiles)

        with sp.Fori(*EXPERTS[0]) as E:
            expert_loads(E)
        sp.wait_ge(flag_done, 1)
        over = sp.value_load(mo["flag"][0:1, 0:1], min_val=0, max_val=1)
        with sp.If(over):
            with sp.Fori(*EXPERTS[1]) as E:
                expert_loads(E)
        for b in range(NB):
            sp.wait_ge(fin_done, b + 1)
            sp.dma_start(out[0, P * b:P * (b + 1), :], hn[:, b, :]).then_inc(s_out, 16)
        sp.wait_ge(s_out, 16 * NB)

    @block.gpsimd
    def _(pool):
        pool.dma_start(ident[:], ident_c).then_inc(s_const, 16)

        def load_gain(i):
            if i >= 2:
                pool.wait_ge(hn_done, NB * (i - 1))
            g = norm_gain[i]
            pool.dma_start(gain[:, i % 2, :], g.partition_broadcast(P).rearrange("p a n -> p (a n)")).then_inc(s_gain[i % 2], 16)

        def rstds(i):
            pool.wait_ge(sq_done, NB * (i + 1))
            nc.gpsimd.tensor_scalar(rstd[:, i], sumsq[:, i], 1.0 / D, EPS, ALU.mult, ALU.add).then_inc(rstd_chain, 1)
            pool.wait_ge(rstd_chain, i + 2)
            nc.gpsimd.tensor_tensor(rstd[:, i], rstd[:, i], half_power[:], ALU.pow).then_inc(rstd_done, 1)

        nc.gpsimd.memset(half_power[:], -0.5).then_inc(rstd_chain, 1)
        load_gain(0)
        load_gain(1)
        rstds(0)
        load_gain(2)
        rstds(1)
        load_gain(3)
        pool.wait_ge(ft_psum, KD)
        pool.dma_start(att["mask"][:], mask_c).then_inc(s_mask, 16)
        pool.dma_start(att["band"][:], band_c).then_inc(s_mask, 16)
        for half in range(2):
            d0 = WIN_H_MAX - 1 - (ROWS - 2) - half
            pool.dma_start(att["table"][RPB_W * half:RPB_W * (half + 1)], rpb[:, :, d0:d0 + SHIFTS]).then_inc(s_mask, 16)

        rstds(2)
        load_gain(4)
        for i in range(HEADS):
            pool.wait_ge(a_inv, i + 1)
            for b in range(NB):
                p = hid[i % 2][:, S * b:S * (b + 1)]
                last = nc.gpsimd.tensor_scalar(p, p, att["p_inv"][:, i % 2, b:b + 1], None, ALU.mult)
            last.then_inc(a_norm, 1)
        rstds(3)
        pool.wait_ge(piece_used, at["wo"][-1][-1] + 1)
        pool.dma_start(mo["rw"][:], router_w[0].rearrange("(k p) n -> p k n", p=P)).then_inc(s_rout, 16)
        pool.dma_start(mo["rb"][:], router_b[0:1, :].partition_broadcast(P).rearrange("p a n -> p (a n)")).then_inc(s_rout, 16)
        pool.dma_start(mo["before"][:], before_c).then_inc(s_rout, 16)
        pool.dma_start(mo["count"][:], count_c).then_inc(s_rout, 16)
        nc.gpsimd.memset(mo["ones"][:], 1.0).then_inc(ones_done, 1)
        nc.gpsimd.memset(mo["slot"][:], -1.0).then_inc(ones_done, 1)
        rstds(4)

    @block.scalar
    def _(act):
        made = [0]

        def split_hi(j, E):
            s, w = slot_of(j, E, RAW), slot_of(j, E, SPLIT)
            rounds = 16 * (j // RAW + 1) if E is None else 16 * ((N0 + j) // RAW + 1) + E * (16 * PER_EXPERT // RAW)
            act.wait_ge(raw_in[s], rounds)
            if has_before(j, E, SPLIT):
                act.wait_ge(piece_used, piece(j, E, SPLIT))
            nc.scalar.activation(w_hi[w][:], raw[s][:], ACT.Copy).then_inc(hi_made, 1)

        def split_past(n):
            while made[0] < min(n + SPLIT, N1):
                split_hi(made[0], None)
                made[0] += 1

        whole = [(s_x, 16), (h_ready, 1), (d_added, NB * DC), (h_ready, 2), (moe_done, 1)]

        def squares(i):
            act.wait_ge(*whole[i])
            for b in range(NB):
                nc.scalar.activation(hn[:, b], h[:, b], ACT.Square, accum_out=sumsq[:, i, b:b + 1]).then_inc(sq_done, 1)

        def norm_to_act(i):
            squares(i)
            for q in range(4):
                act.wait_ge(tr_done, 4 * i + q + 1)
                nc.scalar.activation(act_hi[:, 2 * q:2 * q + 2], two(TY[q]), ACT.Copy).then_inc(act_hi_done, 1)

        def copy_groups(n, source, hi, ready, done):
            for q in range(n):
                act.wait_ge(ready, q + 1)
                nc.scalar.activation(hi(q), source(q), ACT.Copy).then_inc(done, 1)

        split_past(0)
        norm_to_act(0)
        act.wait_ge(s_dft, 16)
        nc.scalar.activation(fo["dft_hi"][:], fo["dft_raw"][:], ACT.Copy).then_inc(dft_hi_done, 1)
        for c in range(2):
            split_past(at["w_in"][c][-1])
            for b in range(NB):
                projected(act, u_psum, c, at["w_in"][c], b)
                nc.scalar.activation(fo["u_hi"][:, b, BANK * c:BANK * (c + 1)], (G, U)[c][b][:], ACT.Copy).then_inc(u_hi_done, 1)
        copy_groups(KD, lambda m: TY[m % 4][:], lambda m: fo["pt_hi"][:, m], pt_psum, pt_hi_done)
        copy_groups(KD, lambda m: TY[m % 4][:, :S], lambda m: act_hi[:, m], ft_psum, ft_hi_done)
        for c in range(2):
            split_past(at["w_out"][c][-1])
        split_past(at["w_out"][-1][-1] + 1)
        norm_to_act(1)
        def dense_hidden_hi(c):
            for b in range(NB):
                act.wait_ge(d_hidT, NB * c + b + 1)
                if c:
                    projected(act, d_down, c - 1, at["down"][c - 1], b)
                nc.scalar.activation(hidT_hi[b][:, :widths[c]], T[b][:, :widths[c]], ACT.Copy).then_inc(d_hidT_hi, 1)

        for c in range(DC):
            w = widths[c]
            split_past(at["gate"][c][-1])
            for b in range(NB):
                projected(act, d_gate, c, at["gate"][c], b)
                if c:
                    act.wait_ge(d_hid, NB * (c - 1) + b + 1)
                nc.scalar.activation(silu_g[b][:, :w], G[b][:, :w], ACT.Silu).then_inc(d_silu, 1)
            if c:
                dense_hidden_hi(c - 1)
            split_past(at["up"][c][-1])
            if c:
                split_past(at["down"][c - 1][-1])
        dense_hidden_hi(DC - 1)
        split_past(at["down"][-1][-1] + 1)
        norm_to_act(2)
        for c in range(6):
            split_past(at["qkv"][c][-1])
            projected(act, qkv_psum, c, at["qkv"][c], 0)
            if 2 <= c < 4:
                act.wait_ge(qkT_psum, 2 * (c - 1))
            dst = att["qk"][:, c % 2, 0] if c < 4 else att["v"][:, 0, BANK * (c - 4):BANK * (c - 3)]
            nc.scalar.activation(dst, (G, U)[c % 2][0][:], ACT.Copy).then_inc(qkv_act, 1)
            if 1 <= c < 5:
                act.wait_ge(qkT_psum, 2 * c - 1)
                dst = att["qT"] if c < 3 else att["kT"]
                m = 4 * ((c - 1) % 2)
                nc.scalar.activation(dst[:, m:m + 2], two((T, Y)[(c - 1) % 2][0]), ACT.Copy).then_inc(qT_act, 1)
        for i in range(HEADS + 4):
            if i < HEADS:
                act.wait_ge(a_max, i + 1)
                if i >= 2:
                    act.wait_ge(a_pT, i - 1)
                for b in range(NB):
                    last = nc.scalar.activation(hid[i % 2][:, S * b:S * (b + 1)], silu_g[i % 2][:, S * b:S * (b + 1)],
                                                ACT.Exp, bias=att["neg_max"][:, i % 2, b:b + 1],
                                                accum_out=att["p_sum"][:, i % 2, b:b + 1])
                    last.then_inc(a_exp, 1)
            if 2 <= i < HEADS + 2:
                g = i - 2
                act.wait_ge(a_pT, g + 1)
                if g >= 2:
                    act.wait_ge(a_pv, g - 1)
                nc.scalar.activation(att["probT"][:, g % 2], T[g % 2][:], ACT.Copy).then_inc(a_pTcopy, 1)
            if i >= 4 and i % 2 == 0:
                m = (i - 4) // 2
                act.wait_ge(a_pv, 2 * m + 2)
                nc.scalar.activation(act_hi[:, m], Y[m % 2][:, :S], ACT.Copy).then_inc(a_ohi, 1)
        for c in range(2):
            split_past(at["wo"][c][-1] + 1)
        norm_to_act(3)
        act.wait_ge(hn_done, NB * 4)
        nc.scalar.activation(mo["hn_hi"][:], hn[:], ACT.Copy).then_inc(hnr_hi, 1)
        act.wait_ge(s_rout, 64)
        nc.scalar.activation(mo["rw_hi"][:], mo["rw"][:], ACT.Copy).then_inc(rw_hi_done, 1)
        act.wait_ge(gap_done, 1)
        nc.scalar.activation(mo["ratio"][:], mo["gap"][:], ACT.Exp).then_inc(ratio_done, 1)

        def gather_hi(E1):
            act.wait_ge(e_gather, E1)
            for q in range(2):
                last = nc.scalar.activation(mo["xg_hi"][:, 4 * q:4 * q + 4], four((G, U)[q][1]), ACT.Copy)
            last.then_inc(e_xhi, 1)

        def silu(E, c):
            act.wait_ge(piece_used, piece(AT["gate", c, 1], E))
            if c != 1:
                act.wait_ge(e_hid, E * STEPS + max(c - 1, 0))
            nc.scalar.activation(silu_g[c % 2][:], G[c % 2][:], ACT.Silu).then_inc(e_silu, 1)

        def hidden_hi(E, c):
            act.wait_ge(e_hidT, E * STEPS + (c + 1))
            if c != 1:
                act.wait_ge(piece_used, piece(AT["down", c - 2, 1] if c else -1, E))
            nc.scalar.activation(hidT_hi[c % 2][:], T[c % 2][:], ACT.Copy).then_inc(e_hidT_hi, 1)

        def result_hi(E):
            act.wait_ge(piece_used, piece(PER_EXPERT - 1, E))
            for q in range(2):
                last = nc.scalar.activation(mo["y_hi"][:, BANK * q:BANK * (q + 1)], Y[q][:], ACT.Copy)
            last.then_inc(e_yhi, 1)

        def expert(E, sweep):
            for j, (kind, c, half) in enumerate(EXPERT):
                if (kind, half) == ("gate", 1):
                    silu(E, c)
                    if c:
                        hidden_hi(E, c - 1)
                if (kind, c, half) == ("up", STEPS - 1, 1):
                    gather_hi(E + (sweep + 2))
                if (kind, c, half) == ("down", STEPS - 2, 0):
                    hidden_hi(E, STEPS - 1)
                if (kind, c, half) == ("down", STEPS - 1, 1):
                    result_hi(E)
                split_hi(j + SPLIT, E)

        gather_hi(1)
        with act.Fori(*EXPERTS[0]) as E:
            expert(E, 0)
        act.wait_ge(flag_done, 1)
        over = act.value_load(mo["flag"][0:1, 0:1], min_val=0, max_val=1)
        with act.If(over):
            gather_hi(NE + 2)
            with act.Fori(*EXPERTS[1]) as E:
                expert(E, 1)
        squares(4)

    @block.vector
    def _(dve):
        made = [0]
        chain = [0]

        def link(ins):
            chain[0] += 1
            ins.then_inc(dve_chain, 1)
            dve.wait_ge(dve_chain, chain[0])

        def split_lo(j, E):
            s, w = slot_of(j, E, RAW), slot_of(j, E, SPLIT)
            dve.wait_ge(hi_made, piece(j, E))
            nc.vector.tensor_tensor(w_lo[w][:], raw[s][:], w_hi[w][:].bitcast(f32), ALU.subtract).then_inc(lo_made, 1)

        def split_past(n):
            while made[0] < min(n + SPLIT, N1):
                split_lo(made[0], None)
                made[0] += 1

        def rest(out_, whole, hi):
            return nc.vector.tensor_tensor(out_, whole, hi.bitcast(f32), ALU.subtract)

        def normalise(i, b):
            nc.vector.scalar_tensor_tensor(out=hn[:, b], in0=h[:, b], scalar=rstd[:, i, b:b + 1], in1=gain[:, i % 2],
                                           op0=ALU.mult, op1=ALU.mult).then_inc(hn_done if i < 4 else fin_done, 1)

        def norm_to_act(i):
            dve.wait_ge(rstd_done, i + 1)
            dve.wait_ge(s_gain[i % 2], 16 * (i // 2 + 1))
            for b in range(NB):
                normalise(i, b)
            for q in range(4):
                dve.wait_ge(act_hi_done, 4 * i + q + 1)
                rest(act_lo[:, 2 * q:2 * q + 2], two(TY[q]),
                     act_hi[:, 2 * q:2 * q + 2]).then_inc(act_lo_done, 1)

        def add_projection(pieces, psum, i):
            for c in range(2):
                split_past(pieces[c][-1])
                for b in range(NB):
                    projected(dve, psum, c, pieces[c], b)
                    part = h[:, b, BANK * c:BANK * (c + 1)]
                    last = nc.vector.tensor_tensor(part, (G, U)[c][b][:], part, ALU.add)
            last.then_inc(h_ready, 1)
            split_past(pieces[-1][-1] + 1)

        split_past(0)
        norm_to_act(0)
        dve.wait_ge(dft_hi_done, 1)
        rest(fo["dft_lo"][:], fo["dft_raw"][:], fo["dft_hi"][:]).then_inc(dft_lo_done, 1)
        for c in range(2):
            split_past(at["w_in"][c][-1])
            for b in range(NB):
                dve.wait_ge(u_hi_done, NB * c + b + 1)
                cs = slice(BANK * c, BANK * (c + 1))
                rest(fo["u_lo"][:, b, cs], (G, U)[c][b][:], fo["u_hi"][:, b, cs]).then_inc(u_lo_done, 1)
        for m in range(KD):
            dve.wait_ge(pt_hi_done, m + 1)
            rest(fo["pt_lo"][:, m], TY[m % 4][:], fo["pt_hi"][:, m]).then_inc(pt_lo_done, 1)
        for m in range(KD):
            dve.wait_ge(ft_hi_done, m + 1)
            rest(act_lo[:, m], TY[m % 4][:, :S], act_hi[:, m]).then_inc(ft_lo_done, 1)
        add_projection(at["w_out"], fo_psum, 0)
        norm_to_act(1)

        def hidden_lo(c):
            for b in range(NB):
                dve.wait_ge(d_hidT_hi, NB * c + b + 1)
                rest(hidT_lo[b][:, :widths[c]], T[b][:, :widths[c]], hidT_hi[b][:, :widths[c]]).then_inc(d_hidT_lo, 1)

        def add_down(c):
            for b in range(NB):
                projected(dve, d_down, c, at["down"][c], b)
                for q in range(2):
                    part = h[:, b, BANK * q:BANK * (q + 1)]
                    last = nc.vector.tensor_tensor(part, (Y, T)[b][q][:], part, ALU.add)
                last.then_inc(d_added, 1)

        for c in range(DC):
            w = widths[c]
            split_past(at["gate"][c][-1])
            if c:
                hidden_lo(c - 1)
            split_past(at["up"][c][-1])
            for b in range(NB):
                dve.wait_ge(d_silu, NB * c + b + 1)
                projected(dve, d_up, c, at["up"][c], b)
                if c:
                    dve.wait_ge(d_hidT, NB * (c - 1) + b + 1)
                nc.vector.tensor_tensor(hid[b][:, :w], U[b][:, :w], silu_g[b][:, :w], ALU.mult).then_inc(d_hid, 1)
            if c:
                split_past(at["down"][c - 1][-1])
                add_down(c - 1)
        hidden_lo(DC - 1)
        split_past(at["down"][-1][-1])
        add_down(DC - 1)
        split_past(at["down"][-1][-1] + 1)
        dve.wait_ge(s_mask, 64)
        for n, w0 in enumerate(range(0, GRID, BIAS_W)):
            nw = min(BIAS_W, GRID - w0)
            dve.wait_ge(bias_psum, n + 1)
            full = [P, HEADS * SHIFTS, nw]
            nc.vector.tensor_tensor(att["bias"][:, :, :, w0:w0 + nw].rearrange("p h s w -> p (h s) w"),
                                    GU[n % 4][:, :HEADS * SHIFTS * nw].rearrange("p (w x) -> p x w", w=nw),
                                    att["mask"][:, w0:w0 + nw].unsqueeze(1).to_broadcast(full), ALU.add).then_inc(bias_done, 1)
        norm_to_act(2)
        for c in range(6):
            split_past(at["qkv"][c][-1])
            projected(dve, qkv_psum, c, at["qkv"][c], 1)
            if 2 <= c < 4:
                dve.wait_ge(qkT_psum, 2 * (c - 1))
            dst = att["qk"][:, c % 2, 1] if c < 4 else att["v"][:, 1, BANK * (c - 4):BANK * (c - 3)]
            nc.vector.tensor_copy(dst, (G, U)[c % 2][1][:]).then_inc(qkv_dve, 1)
            if 1 <= c < 5:
                dve.wait_ge(qkT_psum, 2 * c)
                dst = att["qT"] if c < 3 else att["kT"]
                m = 4 * ((c - 1) % 2)
                nc.vector.tensor_copy(dst[:, m + 2:m + 4], two((T, Y)[(c - 1) % 2][1])).then_inc(qT_dve, 1)
        def head_bias(i):
            a = att["bias"][:, i]
            return bass.AP(a.tensor, a.offset, [a.ap[0], [(ROWS - 2) * GRID, NB], [1, S]])

        dve.wait_ge(bias_done, -(-GRID // BIAS_W))
        for i in range(HEADS + 4):
            if i < HEADS:
                dve.wait_ge(a_score, i + 1)
                if i >= 2:
                    dve.wait_ge(a_exp, NB * (i - 1))
                nc.vector.scalar_tensor_tensor(out=silu_g[i % 2][:].rearrange("p (n k) -> p n k", n=NB), in0=two(GU[i % 4]), scalar=float(HD) ** -0.5,
                                               in1=head_bias(i), op0=ALU.mult,
                                               op1=ALU.add).then_inc(a_biased, 1)
                dve.wait_ge(a_biased, i + 1)
                nc.vector.tensor_reduce(att["neg_max"][:, i % 2], silu_g[i % 2][:].rearrange("p (b k) -> p b k", b=NB),
                                        AX.X, ALU.max, negate=True).then_inc(a_max, 1)
            if 1 <= i < HEADS + 1:
                g = i - 1
                dve.wait_ge(a_exp, NB * (g + 1))
                if g >= 2:
                    dve.wait_ge(a_norm, g - 1)
                nc.vector.reciprocal(att["p_inv"][:, g % 2], att["p_sum"][:, g % 2]).then_inc(a_inv, 1)
            if i >= 4 and i % 2 == 0:
                m = (i - 4) // 2
                dve.wait_ge(a_ohi, m + 1)
                rest(act_lo[:, m], Y[m % 2][:, :S], act_hi[:, m]).then_inc(a_olo, 1)
        add_projection(at["wo"], ao_psum, 2)
        norm_to_act(3)

        dve.wait_ge(hnr_hi, 1)
        rest(mo["hn_lo"][:], hn[:], mo["hn_hi"][:]).then_inc(hnr_lo, 1)
        dve.wait_ge(rw_hi_done, 1)
        rest(mo["rw_lo"][:], mo["rw"][:], mo["rw_hi"][:]).then_inc(rw_lo_done, 1)
        dve.wait_ge(logit_psum, 1)
        full = [P, NB, NE]

        def each_token(t):
            return t.unsqueeze(2).to_broadcast(full)

        iota = mo["count"][:, 0:NE].unsqueeze(1).to_broadcast(full)
        link(nc.vector.tensor_tensor(mo["logit"][:], G[0][:, 0:NB * NE].rearrange("p (b e) -> p b e", b=NB),
                                     mo["rb"][:].unsqueeze(1).to_broadcast(full), ALU.add))
        for n, (src, one) in enumerate((("logit", "first"), ("rest", "second"))):
            link(nc.vector.tensor_reduce(mo["top"][:, n], mo[src][:], AX.X, ALU.max))
            link(nc.vector.tensor_tensor(mo["eq"][:], mo[src][:], each_token(mo["top"][:, n]), ALU.is_equal))
            link(nc.vector.scalar_tensor_tensor(out=mo["cand"][:], in0=iota, scalar=-float(NE), in1=mo["eq"][:],
                                                op0=ALU.add, op1=ALU.mult))
            link(nc.vector.tensor_reduce(mo["idx"][:, n], mo["cand"][:], AX.X, ALU.min))
            link(nc.vector.tensor_scalar(mo["idx"][:, n], mo["idx"][:, n], float(NE), None, ALU.add))
            link(nc.vector.tensor_tensor(mo[one][:], iota, each_token(mo["idx"][:, n]), ALU.is_equal))
            if n == 0:
                link(nc.vector.scalar_tensor_tensor(out=mo["rest"][:], in0=mo["first"][:], scalar=-3e38,
                                                    in1=mo["logit"][:], op0=ALU.mult, op1=ALU.add))
        nc.vector.tensor_tensor(mo["used"][:], mo["first"][:], mo["second"][:], ALU.add).then_inc(used_done, 1)
        nc.vector.tensor_tensor(mo["gap"][:], mo["top"][:, 1], mo["top"][:, 0], ALU.subtract).then_inc(gap_done, 1)
        dve.wait_ge(used_done, 1)
        dve.wait_ge(ratio_done, 1)
        link(nc.vector.tensor_scalar(mo["den"][:], mo["ratio"][:], 1.0, None, ALU.add))
        link(nc.vector.reciprocal(mo["g1"][:], mo["den"][:]))
        link(nc.vector.tensor_tensor(mo["g2"][:], mo["ratio"][:], mo["g1"][:], ALU.mult))
        link(nc.vector.tensor_tensor(mo["first"][:], mo["first"][:], each_token(mo["g1"][:]), ALU.mult))
        link(nc.vector.tensor_tensor(mo["second"][:], mo["second"][:], each_token(mo["g2"][:]), ALU.mult))
        link(nc.vector.tensor_tensor(mo["weight"][:], mo["first"][:], mo["second"][:], ALU.add))
        dve.wait_ge(rank_psum, 1)
        dve.wait_ge(ones_done, 2)
        slots = mo["slot"][:, :, 0:NE]
        link(nc.vector.scalar_tensor_tensor(out=slots, in0=G[1][:, 0:NB * NE].rearrange("p (b e) -> p b e", b=NB),
                                            scalar=1.0, in1=mo["used"][:], op0=ALU.add, op1=ALU.mult))
        link(nc.vector.tensor_scalar(slots, slots, -1.0, None, ALU.add))
        link(nc.vector.tensor_reduce(mo["most"][:], G[1][:, NB * NE:(NB + 1) * NE], AX.X, ALU.max))
        nc.vector.tensor_scalar(mo["flag"][:], mo["most"][:], float(P), None, ALU.is_gt).then_inc(flag_done, 1)

        def select(sweep, e):
            for b in range(NB):
                last = nc.vector.tensor_scalar(mo["sel"][:, b], mo["count"][:, P * sweep:P * (sweep + 1)],
                                               mo["slot"][:, b, bass.ds(e, 1)], None, ALU.is_equal)
            last.then_inc(e_sel, 1)

        def gather_lo(E1):
            dve.wait_ge(e_xhi, E1)
            for q in range(2):
                last = rest(mo["xg_lo"][:, 4 * q:4 * q + 4], four((G, U)[q][1]),
                            mo["xg_hi"][:, 4 * q:4 * q + 4])
            last.then_inc(e_xlo, 1)

        def hidden(E, c):
            dve.wait_ge(e_silu, E * STEPS + (c + 1))
            dve.wait_ge(piece_used, piece(AT["up", c, 1], E))
            if c != 1:
                dve.wait_ge(e_hidT, E * STEPS + max(c - 1, 0))
            nc.vector.tensor_tensor(hid[c % 2][:], U[c % 2][:], silu_g[c % 2][:], ALU.mult).then_inc(e_hid, 1)

        def hidden_rest(E, c):
            dve.wait_ge(e_hidT_hi, E * STEPS + (c + 1))
            rest(hidT_lo[c % 2][:], T[c % 2][:], hidT_hi[c % 2][:]).then_inc(e_hidT_lo, 1)

        def next_selection(E, e, sweep):
            dve.wait_ge(e_selT, E + 1)
            dve.wait_ge(e_scatter, E)
            nc.vector.tensor_copy(mo["selT"][:], T[1][:, :NB * P].rearrange("p (b t) -> p b t", b=NB)).then_inc(e_selT_copy, 1)
            select(sweep, e + 1)

        def result_rest(E):
            dve.wait_ge(e_yhi, E + 1)
            for q in range(2):
                cs = slice(BANK * q, BANK * (q + 1))
                last = rest(mo["y_lo"][:, cs], Y[q][:], mo["y_hi"][:, cs])
            last.then_inc(e_ylo, 1)

        def add_result(E, e):
            dve.wait_ge(e_scatter, E + 1)
            for b in range(NB):
                for q in range(2):
                    part = h[:, b, BANK * q:BANK * (q + 1)]
                    src = T[q] if b == 0 else (G, U)[q][1]
                    last = nc.vector.scalar_tensor_tensor(out=part, in0=src[:], scalar=mo["weight"][:, b, bass.ds(e, 1)],
                                                          in1=part, op0=ALU.mult, op1=ALU.add)
            last.then_inc(e_added, 1)

        def expert(E, sweep):
            e = E - NE if sweep else E
            for j, (kind, c, half) in enumerate(EXPERT):
                if (kind, c, half) == ("gate", 0, 1):
                    next_selection(E, e, sweep)
                elif (kind, half) == ("gate", 1):
                    hidden_rest(E, c - 1)
                if (kind, half) == ("up", 1):
                    hidden(E, c)
                    if c == STEPS - 1:
                        gather_lo(E + (sweep + 2))
                if (kind, c, half) == ("down", STEPS - 2, 0):
                    hidden_rest(E, STEPS - 1)
                if (kind, c, half) == ("down", STEPS - 1, 1):
                    result_rest(E)
                    add_result(E, e)
                split_lo(j + SPLIT, E)

        dve.wait_ge(dve_chain, chain[0])
        select(0, 0)
        gather_lo(1)
        with dve.Fori(*EXPERTS[0]) as E:
            expert(E, 0)
        dve.wait_ge(flag_done, 1)
        over = dve.value_load(mo["flag"][0:1, 0:1], min_val=0, max_val=1)
        with dve.If(over):
            dve.wait_ge(e_gather, NE + 1)
            select(1, 0)
            gather_lo(NE + 2)
            with dve.Fori(*EXPERTS[1]) as E:
                expert(E, 1)
            dve.wait_ge(e_added, 2 * NE)
        dve.wait_ge(e_added, NE)
        dve.sem_inc(moe_done, 1)
        dve.wait_ge(rstd_done, 5)
        dve.wait_ge(s_gain[0], 48)
        for b in range(NB):
            normalise(4, b)

    @block.tensor
    def _(pe):
        def ready(j, E):
            pe.wait_ge(lo_made, piece(j, E))

        def parts(j, E, tiles):
            w = slot_of(j, E, SPLIT)
            return [t[:].rearrange("p (k n) -> p k n", k=tiles) for t in (w_hi[w], w_lo[w])]

        def three(out_, xh, xl, wh, wl, start, stop):
            nc.tensor.matmul(out_, xh, wh, start=start, stop=False)
            nc.tensor.matmul(out_, xh, wl, start=False, stop=False)
            return nc.tensor.matmul(out_, xl, wh, start=False, stop=stop)

        def project(pieces, banks, width, done, wait_banks=lambda: None):
            for n, j in enumerate(pieces):
                tiles = PIECE // width
                ready(j, None)
                if n == 0:
                    wait_banks()
                wh, wl = parts(j, None, tiles)
                for b in range(NB):
                    for k in range(tiles):
                        kk = tiles * n + k
                        last = three(banks[b][:, :width], act_hi[:, kk, P * b:P * (b + 1)], act_lo[:, kk, P * b:P * (b + 1)],
                                     wh[:, k], wl[:, k], kk == 0, kk == KD - 1)
                    if n == len(pieces) - 1 and b < NB - 1:
                        last.then_inc(done, 1)
                last.then_inc(piece_used, 1)

        def transpose_stream(i):
            for q in range(4):
                if q == 0:
                    pe.wait_ge(hn_done, NB * (i + 1))
                    if i == 0:
                        pe.wait_ge(s_const, 16)
                bk = TY[q]
                for k in range(2):
                    for b in range(NB):
                        o = S * k + P * b
                        kk = 2 * q + k
                        last = nc.tensor.transpose(bk[:, o:o + P], hn[:, b, P * kk:P * (kk + 1)], ident[:])
                last.then_inc(tr_done, 1)
            pe.wait_ge(act_lo_done, 4 * (i + 1))

        transpose_stream(0)
        for c in range(2):
            project(at["w_in"][c], (G, U)[c], BANK, u_psum)
        pe.wait_ge(dft_lo_done, 1)
        for m in range(KD):
            if m == 0:
                pe.wait_ge(u_lo_done, NB)
            if m == KD // 2:
                pe.wait_ge(u_lo_done, 2 * NB)
            if m >= 4:
                pe.wait_ge(pt_lo_done, m - 3)
            bk = TY[m % 4]
            for b in range(NB):
                last = three(bk[:], fo["u_hi"][:, b, P * m:P * (m + 1)], fo["u_lo"][:, b, P * m:P * (m + 1)],
                             fo["dft_hi"][:, b, 0:2 * S], fo["dft_lo"][:, b, 0:2 * S], b == 0, b == NB - 1)
            last.then_inc(pt_psum, 1)
        for m in range(KD):
            g0 = m // 2 * 2
            pe.wait_ge(pt_lo_done, KD if m >= 4 else max(g0 + 2, m + 5))
            if m >= 4:
                pe.wait_ge(ft_lo_done, m - 3)
            bk = TY[m % 4]
            terms = [(k, part) for k in range(2) for part in range(2)]
            for n, (k, part) in enumerate(terms):
                o = (0, 2 * S)[part] + P * (m % 2)
                last = three(bk[:, :S], fo["dft_hi"][:, k, o:o + P], fo["dft_lo"][:, k, o:o + P],
                             fo["pt_hi"][:, g0 + k, S * part:S * (part + 1)], fo["pt_lo"][:, g0 + k, S * part:S * (part + 1)],
                             n == 0, n == len(terms) - 1)
            last.then_inc(ft_psum, 1)
        pe.wait_ge(ft_lo_done, KD)
        for c in range(2):
            project(at["w_out"][c], (G, U)[c], BANK, fo_psum)

        transpose_stream(1)

        def hidden_transposes(c):
            for b in range(NB):
                pe.wait_ge(d_hid, NB * c + b + 1)
                if c:
                    pe.wait_ge(d_added, NB * c)
                for k in range(widths[c] // P):
                    last = nc.tensor.transpose(T[b][:, P * k:P * (k + 1)], hid[b][:, P * k:P * (k + 1)], ident[:])
                last.then_inc(d_hidT, 1)

        def down(c):
            pieces = at["down"][c]
            for j in pieces:
                ready(j, None)
            if c:
                pe.wait_ge(d_added, NB * c)
            for b in range(NB):
                if b == 0:
                    pe.wait_ge(d_hidT_lo, NB * (c + 1))
                for n, j in enumerate(pieces):
                    wh, wl = parts(j, None, KROW)
                    for k in range(KROW):
                        kk = KROW * n + k
                        for q in range(2):
                            cs = slice(BANK * q, BANK * (q + 1))
                            last = three((Y, T)[b][q][:], hidT_hi[b][:, P * kk:P * (kk + 1)], hidT_lo[b][:, P * kk:P * (kk + 1)],
                                         wh[:, k, cs], wl[:, k, cs], kk == 0, kk == KROW * len(pieces) - 1)
                    if b == NB - 1:
                        last.then_inc(piece_used, 1)
                if b < NB - 1:
                    last.then_inc(d_down, 1)

        for c in range(DC):
            def gate_banks():
                if c:
                    pe.wait_ge(d_silu, NB * c)
            def up_banks():
                if c:
                    pe.wait_ge(d_hid, NB * c)
            project(at["gate"][c], G, widths[c], d_gate, gate_banks)
            if c:
                hidden_transposes(c - 1)
            project(at["up"][c], U, widths[c], d_up, up_banks)
            if c:
                down(c - 1)
        hidden_transposes(DC - 1)
        down(DC - 1)

        pe.wait_ge(s_mask, 64)
        for n, w0 in enumerate(range(0, GRID, BIAS_W)):
            if n >= 4:
                pe.wait_ge(bias_done, n - 3)
            else:
                pe.wait_ge(d_hid, NB * DC)
            for w in range(w0, min(w0 + BIAS_W, GRID)):
                o = HEADS * SHIFTS * (w - w0)
                last = nc.tensor.matmul(GU[n % 4][:, o:o + HEADS * SHIFTS], att["band"][:, GRID - 1 - w:P + GRID - 1 - w],
                                        att["table"][:], start=True, stop=True)
            last.then_inc(bias_psum, 1)
        transpose_stream(2)
        pe.wait_ge(bias_done, -(-GRID // BIAS_W))

        def transpose_qk(c):
            pe.wait_ge(qkv_act, c + 1)
            pe.wait_ge(qkv_dve, c + 1)
            if c >= 2:
                pe.wait_ge(qT_act, c - 1)
                pe.wait_ge(qT_dve, c - 1)
            for t in range(2):
                for k in range(2):
                    for b in range(NB):
                        o = S * k + P * b
                        m = 2 * t + k
                        last = nc.tensor.transpose((T, Y)[c % 2][t][:, o:o + P], att["qk"][:, c % 2, b, P * m:P * (m + 1)], ident[:])
                last.then_inc(qkT_psum, 1)

        for c in range(6):
            def qkv_banks():
                if c >= 2:
                    pe.wait_ge(qkv_act, c - 1)
                    pe.wait_ge(qkv_dve, c - 1)
            project(at["qkv"][c], (G, U)[c % 2], BANK, qkv_psum, qkv_banks)
            if 1 <= c < 5:
                transpose_qk(c - 1)
        pe.wait_ge(qkv_act, 6)
        pe.wait_ge(qkv_dve, 6)
        pe.wait_ge(qT_act, 4)
        pe.wait_ge(qT_dve, 4)
        for i in range(HEADS + 3):
            if i < HEADS:
                m, p0 = i // 2, HD * (i % 2)
                if i >= 4:
                    pe.wait_ge(a_biased, i - 3)
                for b in range(NB):
                    n = NB - 1 - b
                    last = nc.tensor.matmul(GU[i % 4][:, S * n:S * (n + 1)], att["qT"][p0:p0 + HD, m, P * b:P * (b + 1)],
                                            att["kT"][p0:p0 + HD, m, :], start=True, stop=True)
                last.then_inc(a_score, 1)
            if 2 <= i < HEADS + 2:
                g = i - 2
                pe.wait_ge(a_norm, g + 1)
                if g >= 2:
                    pe.wait_ge(a_pTcopy, g - 1)
                for k in range(NB):
                    for b in range(NB):
                        o, n = S * k + P * b, NB - 1 - b
                        last = nc.tensor.transpose(T[g % 2][:, o:o + P], hid[g % 2][:, S * n + P * k:S * n + P * (k + 1)], ident[:])
                last.then_inc(a_pT, 1)
            if i >= 3:
                g = i - 3
                m, p0 = g // 2, HD * (g % 2)
                pe.wait_ge(a_pTcopy, g + 1)
                if m >= 2 and g % 2 == 0:
                    pe.wait_ge(a_olo, m - 1)
                for k in range(NB):
                    last = nc.tensor.matmul(Y[m % 2][p0:p0 + HD, 0:S], att["v"][:, k, HD * g:HD * (g + 1)],
                                            att["probT"][:, g % 2, S * k:S * (k + 1)], start=(k == 0), stop=(k == NB - 1))
                last.then_inc(a_pv, 1)
        pe.wait_ge(a_olo, HEADS // 2)
        for c in range(2):
            project(at["wo"][c], (G, U)[c], BANK, ao_psum)

        transpose_stream(3)
        pe.wait_ge(rw_lo_done, 1)
        for b in range(NB):
            for k in range(KD):
                last = three(G[0][:, NE * b:NE * (b + 1)], act_hi[:, k, P * b:P * (b + 1)], act_lo[:, k, P * b:P * (b + 1)],
                             mo["rw_hi"][:, k], mo["rw_lo"][:, k], k == 0, k == KD - 1)
        last.then_inc(logit_psum, 1)
        pe.wait_ge(used_done, 1)
        pe.wait_ge(ones_done, 2)
        pe.wait_ge(s_rout, 64)
        used = mo["used"]
        nc.tensor.matmul(G[1][:, 0:NE], mo["before"][:], used[:, 0], start=True, stop=True)
        nc.tensor.matmul(G[1][:, NE:2 * NE], mo["ones"][:], used[:, 0], start=True, stop=False)
        nc.tensor.matmul(G[1][:, NE:2 * NE], mo["before"][:], used[:, 1], start=False, stop=True)
        nc.tensor.matmul(G[1][:, 2 * NE:3 * NE], mo["ones"][:], used[:, 0], start=True, stop=False)
        nc.tensor.matmul(G[1][:, 2 * NE:3 * NE], mo["ones"][:], used[:, 1], start=False, stop=True).then_inc(rank_psum, 1)

        def gather():
            for k in range(KD):
                o = (G, U)[k // 4][1][:, P * (k % 4):P * (k % 4 + 1)]
                for n, (b, part) in enumerate([(b, part) for b in range(NB) for part in ("hn_hi", "hn_lo")]):
                    last = nc.tensor.matmul(o, mo[part][:, b, P * k:P * (k + 1)], mo["sel"][:, b], start=(n == 0), stop=(n == 3))
            last.then_inc(e_gather, 1)

        def expert(E, sweep):
            def columns(kind, c, bk):
                for half in range(2):
                    j = AT[kind, c, half]
                    ready(j, E)
                    wh, wl = parts(j, E, KH)
                    for k in range(KH):
                        kk = KH * half + k
                        last = three(bk[:], mo["xg_hi"][:, kk], mo["xg_lo"][:, kk], wh[:, k], wl[:, k], kk == 0, kk == KD - 1)
                    last.then_inc(piece_used, 1)

            def hidden_transposes(c):
                pe.wait_ge(e_hid, E * STEPS + (c + 1))
                if c >= 2:
                    pe.wait_ge(e_hidT_lo, E * STEPS + (c - 1))
                if c == 1:
                    pe.wait_ge(e_selT_copy, E + 1)
                for k in range(BANK // P):
                    last = nc.tensor.transpose(T[c % 2][:, P * k:P * (k + 1)], hid[c % 2][:, P * k:P * (k + 1)], ident[:])
                last.then_inc(e_hidT, 1)

            def down(c, half):
                j = AT["down", c, half]
                ready(j, E)
                if half == 0:
                    pe.wait_ge(e_hidT_lo, E * STEPS + (c + 1))
                    if c == 0:
                        pe.wait_ge(e_ylo, E)
                wh, wl = parts(j, E, KROW)
                for k in range(KROW):
                    kk = KROW * half + k
                    for q in range(2):
                        cs = slice(BANK * q, BANK * (q + 1))
                        last = three(Y[q][:], hidT_hi[c % 2][:, P * kk:P * (kk + 1)], hidT_lo[c % 2][:, P * kk:P * (kk + 1)],
                                     wh[:, k, cs], wl[:, k, cs], c == 0 and kk == 0, c == STEPS - 1 and kk == BANK // P - 1)
                last.then_inc(piece_used, 1)

            for c in range(STEPS):
                if c == 0:
                    pe.wait_ge(e_xlo, E + (sweep + 1))
                    pe.wait_ge(e_silu, E * STEPS)
                elif c == 1:
                    pe.wait_ge(e_added, E)
                else:
                    pe.wait_ge(e_silu, E * STEPS + (c - 1))
                columns("gate", c, G[c % 2])
                if c == 0:
                    pe.wait_ge(e_added, E)
                    pe.wait_ge(e_sel, E + (sweep + 1))
                    for b in range(NB):
                        last = nc.tensor.transpose(T[1][:, P * b:P * (b + 1)], mo["sel"][:, b].bitcast(f32), ident[:])
                    last.then_inc(e_selT, 1)
                else:
                    hidden_transposes(c - 1)
                if c != 1:
                    pe.wait_ge(e_hid, E * STEPS + max(c - 1, 0))
                columns("up", c, U[c % 2])
                if 1 <= c < STEPS - 1:
                    down(c - 1, 0)
                    down(c - 1, 1)
            pe.wait_ge(e_sel, E + (sweep + 2))
            pe.wait_ge(e_hid, E * STEPS + (STEPS - 1))
            gather()
            down(STEPS - 2, 0)
            hidden_transposes(STEPS - 1)
            down(STEPS - 2, 1)
            down(STEPS - 1, 0)
            down(STEPS - 1, 1)
            pe.wait_ge(e_ylo, E + 1)
            pe.wait_ge(e_selT_copy, E + 1)
            pe.wait_ge(e_xlo, E + (sweep + 2))
            for b in range(NB):
                for q in range(2):
                    cs = slice(BANK * q, BANK * (q + 1))
                    bk = T[q] if b == 0 else (G, U)[q][1]
                    nc.tensor.matmul(bk[:], mo["selT"][:, b], mo["y_hi"][:, cs], start=True, stop=False)
                    last = nc.tensor.matmul(bk[:], mo["selT"][:, b], mo["y_lo"][:, cs], start=False, stop=True)
            last.then_inc(e_scatter, 1)

        pe.wait_ge(hnr_lo, 1)
        pe.wait_ge(e_sel, 1)
        gather()
        with pe.Fori(*EXPERTS[0]) as E:
            expert(E, 0)
        pe.wait_ge(flag_done, 1)
        over = pe.value_load(mo["flag"][0:1, 0:1], min_val=0, max_val=1)
        with pe.If(over):
            pe.wait_ge(e_added, NE)
            pe.wait_ge(e_sel, NE + 2)
            gather()
            with pe.Fori(*EXPERTS[1]) as E:
                expert(E, 1)

    block.__exit__(None, None, None)


_INS = ["x", "norm_mix", "norm_ffn", "fourier_w_in", "fourier_w_out", "nat_w_qkv", "nat_rpb", "nat_w_o",
        "ffn_w_gate", "ffn_w_up", "ffn_w_down", "router_w", "router_b", "expert_w_gate", "expert_w_up",
        "expert_w_down", "final_norm"]
_OUTS = [((1, S, D), "float32")]


def shape_constants():
    turn = 2 * np.pi * (np.outer(np.arange(S), np.arange(S)) % S) / S
    cos, sin = np.cos(turn) / np.sqrt(S), np.sin(turn) / np.sqrt(S)
    dft = np.concatenate([cos, sin, -sin], 1).astype(np.float32)
    q, k = np.arange(P)[:, None] % GRID, np.arange(GRID)[None, :]
    start = np.clip(q - WIN_W // 2, 0, GRID - WIN_W)
    mask = np.where((k >= start) & (k < start + WIN_W), 0.0, MASKED).astype(np.float32)
    band = np.zeros((2, RPB_W, P + GRID - 1), np.float32)
    j = np.arange(RPB_W)
    for half in range(2):
        band[half, j, GRID * (half + 1) - 1 + WIN_W - 1 - j] = 1.0
    before = np.triu(np.ones((P, P), np.float32), 1)
    count = np.tile(np.arange(S, dtype=np.float32), (P, 1))
    return {"dft": dft, "mask": mask, "band": band.reshape(2 * RPB_W, -1), "ident": np.eye(P, dtype=np.float32), "before": before, "count": count}


def kernel(**inputs):
    import concourse.bacc as bacc
    from concourse.bass_utils import run_bass_kernel_spmd

    nc = bacc.Bacc("TRN2", target_bir_lowering=False, num_devices=1, dynamic_dma_scratch_size=8192)
    arrays, args = {}, []
    inputs["nat_rpb"] = np.transpose(inputs["nat_rpb"][0], (2, 0, 1))
    for name, a in [(n, inputs[n]) for n in _INS] + list(shape_constants().items()):
        a = np.ascontiguousarray(a)
        arrays[f"in_{name}"] = a
        args.append(nc.dram_tensor(f"in_{name}", a.shape, mybir.dt.from_np(a.dtype), kind="ExternalInput").ap())
    for i, (shape, dtype) in enumerate(_OUTS):
        args.append(nc.dram_tensor(f"out_{i}", shape, mybir.dt.from_np(np.dtype(dtype)), kind="ExternalOutput").ap())
    trunk(nc, *args)
    r = run_bass_kernel_spmd(nc, [arrays], core_ids=[0])
    return r.results[0]["out_0"]
```

```python
import concourse.bass as bass
from concourse import mybir
from contextlib import ExitStack
import numpy as np

P = 128
D = 1024
S = 256
NB = S // P
KD = D // P
GRID = 64
ROWS = S // GRID
WIN_W = 16
WIN_H_MAX = 8
HEADS = 16
HD = D // HEADS
GROUP = 256
FF = 2816
FFE = 3584
NE = 8
EPS = 1e-6
BANK = 512
PIECE = 2048
RAW = 6
SPLIT = 3
KH = PIECE // BANK
KROW = PIECE // D
RPB_W = 2 * WIN_W - 1
SHIFTS = 2 * ROWS - 2
BIAS_STEPS = 4
SLIDE = 2 * GRID - 1
MASKED = -1e30


def dense_pieces(w_in, w_out, ffg, ffu, ffd, qkv, wo):
    def columns(w, c0, width=BANK):
        tiles = PIECE // width
        v = w.rearrange("(k p) n -> p k n", p=P)
        return [(v[:, k:k + tiles, c0:c0 + width], tiles, width) for k in range(0, KD, tiles)]

    def rows(w, r0, n_rows):
        v = w.rearrange("(k p) n -> p k n", p=P)
        return [(v[:, k:k + KROW, :], KROW, D) for k in range(r0 // P, (r0 + n_rows) // P, KROW)]

    out = {"w_in": [columns(w_in, c) for c in (0, BANK)], "w_out": [columns(w_out, c) for c in (0, BANK)],
           "qkv": [columns(qkv, c) for c in range(0, 3 * D, BANK)], "wo": [columns(wo, c) for c in (0, BANK)]}
    widths = [BANK] * (FF // BANK) + ([FF % BANK] if FF % BANK else [])
    out["gate"] = [columns(ffg, BANK * c, w) for c, w in enumerate(widths)]
    out["up"] = [columns(ffu, BANK * c, w) for c, w in enumerate(widths)]
    out["down"] = [rows(ffd, BANK * c, w) for c, w in enumerate(widths)]
    order = [x for k in ("w_in", "w_out") for x in out[k]]
    for c in range(len(widths)):
        order += [out["gate"][c], out["up"][c]]
        if c:
            order.append(out["down"][c - 1])
    order.append(out["down"][-1])
    order += out["qkv"] + out["wo"]
    flat = [piece for group in order for piece in group]
    where = {}
    n = 0
    for group in order:
        where[id(group)] = list(range(n, n + len(group)))
        n += len(group)
    index = {k: [where[id(g)] for g in v] for k, v in out.items()}
    return flat, index, widths


STEPS = FFE // BANK
def expert_pieces():
    order = []
    for c in range(STEPS):
        order += [("gate", c, 0), ("gate", c, 1), ("up", c, 0), ("up", c, 1)]
        if c:
            order += [("down", c - 1, 0), ("down", c - 1, 1)]
    order += [("down", STEPS - 1, 0), ("down", STEPS - 1, 1)]
    return order, {x: j for j, x in enumerate(order)}


PT = 4
EXPERT, AT = expert_pieces()
PER_EXPERT = len(EXPERT)
assert PER_EXPERT % RAW == 0 and PER_EXPERT % SPLIT == 0


def expert_source(ewg, ewu, ewd, e, j):
    kind, c, half = EXPERT[j]
    v = {"gate": ewg, "up": ewu, "down": ewd}[kind][0].rearrange("e (k p) n -> p (e k) n", p=P)
    if kind == "down":
        return v[:, bass.ds(e * (FFE // P) + (BANK // P * c + KROW * half), KROW), :], KROW, D
    return v[:, bass.ds(e * KD + KH * half, KH), BANK * c:BANK * (c + 1)], KH, BANK


def trunk(nc, x, norm_mix, norm_ffn, w_in, w_out, w_qkv, w_o, ffg, ffu, ffd, router_w, router_b,
          ewg, ewu, ewd, final_norm, gains_c, slide_c, dft_c, mask_c, ident_c, before_c, count_c, out):
    f32, f32r, i32 = mybir.dt.float32, mybir.dt.float32r, mybir.dt.int32
    ALU, ACT, AX = mybir.AluOpType, mybir.ActivationFunctionType, mybir.AxisListType

    dense, at, widths = dense_pieces(w_in[0], w_out[0], ffg[0], ffu[0], ffd[0], w_qkv[0], w_o[0])
    N0 = len(dense)
    dense += [expert_source(ewg, ewu, ewd, 0, j) for j in range(SPLIT)]
    N1 = len(dense)

    def sb(name, shape, dt=f32):
        return nc.alloc_sbuf_tensor(name, shape, dt)

    raw = [sb(f"raw{i}", [P, PIECE]) for i in range(RAW)]
    w_hi = [sb(f"w_hi{i}", [P, PIECE], f32r) for i in range(SPLIT)]
    w_lo = [sb(f"w_lo{i}", [P, PIECE], f32r) for i in range(SPLIT)]
    h = sb("h", [P, NB, D])
    hn = sb("hn", [P, NB, D])
    gains = sb("gains", [P, 4, KD])
    mask = sb("mask", [P, GRID])
    act_hi = sb("act_hi", [P, KD, S], f32r)
    act_lo = sb("act_lo", [P, KD, S], f32r)
    ident = sb("ident", [P, P])
    sumsq = sb("sumsq", [P, 5, NB])
    rstd = sb("rstd", [P, 5, NB])
    half_power = sb("half_power", [P, NB])
    silu_g = [sb(f"silu_g{i}", [P, BANK]) for i in range(2)]
    hid = [sb(f"hid{i}", [P, BANK]) for i in range(2)]
    hidT_hi = [sb(f"hidT_hi{i}", [P, BANK], f32r) for i in range(2)]
    hidT_lo = [sb(f"hidT_lo{i}", [P, BANK], f32r) for i in range(2)]

    def width_of(shape):
        return -(-4 * int(np.prod(shape[1:])) // 32) * 32

    def layout(entries, off):
        made = {}
        for name, shape, dt in entries:
            made[name] = nc.alloc_sbuf_tensor_at(name, shape, dt, offset=off)
            off += width_of(shape)
        return made

    bias_l = [("bias", [P, HEADS * SHIFTS, GRID], f32)]
    fourier_l = bias_l + [("dft_hi", [P, NB, 3 * S], f32r), ("dft_lo", [P, NB, 3 * S], f32r),
                          ("u_hi", [P, NB, D], f32r), ("u_lo", [P, NB, D], f32r),
                          ("pt_lo", [P, PT, 2 * S], f32r), ("pt_hi", [P, PT, 2 * S], f32r)]
    attn_l = bias_l + [("qk", [P, 2, NB, BANK], f32), ("qT", [P, KD, S], f32), ("kT", [P, KD, S], f32),
                       ("v", [P, NB, D], f32), ("probT", [P, 2, NB * S], f32), ("neg_max", [P, 2, NB], f32),
                       ("p_sum", [P, NB, HEADS], f32), ("p_inv", [P, NB, HEADS], f32)]
    moe_l = [("gain", [P, 2, D], f32), ("hn_hi", [P, NB, D], f32r), ("hn_lo", [P, NB, D], f32r), ("xg_hi", [P, KD, P], f32r),
             ("xg_lo", [P, KD, P], f32r), ("y_hi", [P, D], f32r), ("y_lo", [P, D], f32r), ("sel", [P, NB, P], f32r),
             ("selT", [P, NB, P], f32r), ("rw", [P, KD, NE], f32), ("rw_hi", [P, KD, NE], f32r),
             ("rw_lo", [P, KD, NE], f32r), ("rb", [P, NE], f32), ("count", [P, S], f32), ("before", [P, P], f32),
             ("ones", [P, P], f32), ("logit", [P, NB, NE], f32), ("top", [P, 2, NB], f32), ("eq", [P, NB, NE], f32),
             ("cand", [P, NB, NE], f32), ("idx", [P, 2, NB], f32), ("first", [P, NB, NE], f32),
             ("second", [P, NB, NE], f32), ("rest", [P, NB, NE], f32), ("used", [P, NB, NE], f32),
             ("gap", [P, NB], f32), ("ratio", [P, NB], f32), ("den", [P, NB], f32), ("g1", [P, NB], f32),
             ("g2", [P, NB], f32), ("weight", [P, NB, NE], f32), ("slot", [P, NB, 2 * NE], f32),
             ("most", [P, 1], f32), ("flag", [P, 1], i32)]
    arena_start = -(-nc.sbuf_base // 32) * 32
    sizes = [sum(width_of(shape) for _, shape, _ in l) for l in (fourier_l, attn_l, moe_l)]
    sb("arena", [P, max(sizes) // 4])
    fo, mo = (layout(l, arena_start) for l in (fourier_l, moe_l))
    behind_bias = arena_start + width_of(bias_l[0][1])
    att = layout(attn_l[1:], behind_bias) | {"bias": fo["bias"]}
    bias_raw = layout([("bias_raw", [P, HEADS * SHIFTS, GRID], f32)], behind_bias)["bias_raw"]
    fo |= layout([("dft_raw", [P, NB, 3 * S], f32)], arena_start + sum(width_of(shape) for _, shape, _ in fourier_l[:-1]))

    bank = {n: nc.alloc_psum_tensor(f"bank_{n}", [P, BANK], f32) for n in ("G0", "G1", "U0", "U1", "Y0", "Y1", "T0", "T1")}
    G, U, Y, T = ([bank[f"{n}0"], bank[f"{n}1"]] for n in "GUYT")

    TY = [T[0], T[1], Y[0], Y[1]]
    GU = [G[0], G[1], U[0], U[1]]

    def two(bk):
        return bk[:].rearrange("p (k s) -> p k s", k=2)

    def four(bk):
        return bk[:].rearrange("p (k s) -> p k s", k=4)

    def sem(name):
        return nc.alloc_semaphore(name)

    raw_in = [sem(f"raw_in{i}") for i in range(RAW)]
    hi_made, lo_made, piece_used = sem("hi_made"), sem("lo_made"), sem("piece_used")
    s_const, s_dft, s_mask, s_rout, s_gain, s_out = (sem(f"s_{n}") for n in ("const", "dft", "mask", "rout", "gain", "out"))
    s_bias = [sem(f"s_bias{step}") for step in range(BIAS_STEPS)]
    s_x = [sem(f"s_x{c}") for c in range(2)]
    h_half, sq_done, rstd_chain, rstd_done, hn_scaled, hn_done = (sem(n) for n in (
        "h_half", "sq_done", "rstd_chain", "rstd_done", "hn_scaled", "hn_done"))
    tr_done, act_hi_done, act_lo_done = sem("tr_done"), sem("act_hi_done"), sem("act_lo_done")
    dft_hi_done, dft_lo_done, u_psum, u_hi_done, u_lo_done = (sem(n) for n in ("dft_hi_done", "dft_lo_done", "u_psum", "u_hi_done", "u_lo_done"))
    pt_psum, pt_hi_done, pt_lo_done, ft_psum, ft_hi_done, ft_lo_done, fo_psum = (sem(n) for n in (
        "pt_psum", "pt_hi_done", "pt_lo_done", "ft_psum", "ft_hi_done", "ft_lo_done", "fo_psum"))
    d_gate, d_silu, d_up, d_hid, d_hidT, d_hidT_hi, d_hidT_lo, d_down, d_added = (sem("d_" + n) for n in (
        "gate", "silu", "up", "hid", "hidT", "hidT_hi", "hidT_lo", "down", "added"))
    qkv_psum, qkv_act, qkv_dve, qkT_psum, qT_act, qT_dve = (sem(n) for n in (
        "qkv_psum", "qkv_act", "qkv_dve", "qkT_psum", "qT_act", "qT_dve"))
    bias_done, a_score, a_biased, a_max, a_exp, a_inv, a_pT, a_pTcopy, a_pv, a_out, a_oT, a_ohi, a_olo, ao_psum = (sem(n) for n in (
        "bias_done", "a_score", "a_biased", "a_max", "a_exp", "a_inv", "a_pT", "a_pTcopy", "a_pv", "a_out", "a_oT", "a_ohi", "a_olo", "ao_psum"))
    hnr_hi, hnr_lo, rw_hi_done, rw_lo_done, ones_done, logit_psum, gap_done, ratio_done, used_done, rank_psum, flag_done, dve_chain = (sem(n) for n in (
        "hnr_hi", "hnr_lo", "rw_hi_done", "rw_lo_done", "ones_done", "logit_psum", "gap_done", "ratio_done", "used_done", "rank_psum", "flag_done", "dve_chain"))
    e_silu, e_hid, e_hidT, e_hidT_hi, e_hidT_lo, e_selT, e_selT_copy, e_sel, e_gather, e_xhi, e_xlo, e_yhi, e_ylo, e_scatter, e_added = (
        sem("e_" + n) for n in ("silu", "hid", "hidT", "hidT_hi", "hidT_lo", "selT", "selT_copy",
                                "sel", "gather", "xhi", "xlo", "yhi", "ylo", "scatter", "added"))
    moe_done, fin_done = sem("moe_done"), sem("fin_done")

    NLAST = at["wo"][-1][-1]
    DC = len(widths)
    EXPERTS = {0: (0, NE), 1: (NE, 2 * NE)}

    def piece(j, E, back=0):
        return j + 1 - back if E is None else E * PER_EXPERT + (N0 + j + 1 - back)

    def slot_of(j, E, n):
        return (j if E is None else N0 + j) % n

    def has_before(j, E, back):
        return E is not None or j >= back

    STREAM = [TY, TY, [U[0], U[1], T[0], Y[0]], TY]
    OB = [U, Y]

    def HT(c):
        return G if c == DC - 1 else T

    def projected(eng, first_block, c, pieces, b):
        if b < NB - 1:
            eng.wait_ge(first_block, c + 1)
        else:
            eng.wait_ge(piece_used, pieces[-1] + 1)

    block = nc.Block()
    block.__enter__()

    @block.sync
    def _(sp):
        def load(j, E, src, tiles):
            s = slot_of(j, E, RAW)
            if has_before(j, E, RAW):
                sp.wait_ge(lo_made, piece(j, E, RAW))
            sp.dma_start(raw[s][:].rearrange("p (k n) -> p k n", k=tiles), src).then_inc(raw_in[s], 16)

        for c in range(2):
            cs = slice(BANK * c, BANK * (c + 1))
            sp.dma_start(h[:, :, cs], x[0, :, cs].rearrange("(b p) d -> p b d", p=P)).then_inc(s_x[c], 16)
        for j, (src, tiles, _) in enumerate(dense):
            load(j, None, src, tiles)
            if j == 3:
                sp.dma_start(fo["dft_raw"][:], dft_c.rearrange("(b p) n -> p b n", p=P)).then_inc(s_dft, 16)

        def expert_loads(E):
            for j in range(SPLIT, PER_EXPERT + SPLIT):
                e = E % NE if j < PER_EXPERT else (E + 1) % NE
                src, tiles, _ = expert_source(ewg, ewu, ewd, e, j % PER_EXPERT)
                load(j, E, src, tiles)

        with sp.Fori(*EXPERTS[0]) as E:
            expert_loads(E)
        sp.wait_ge(flag_done, 1)
        over = sp.value_load(mo["flag"][0:1, 0:1], min_val=0, max_val=1)
        with sp.If(over):
            with sp.Fori(*EXPERTS[1]) as E:
                expert_loads(E)
        for b in range(NB):
            sp.wait_ge(fin_done, b + 1)
            sp.dma_start(out[0, P * b:P * (b + 1), :], hn[:, b, :]).then_inc(s_out, 16)
        sp.wait_ge(s_out, 16 * NB)

    @block.gpsimd
    def _(pool):
        def rstds(i):
            pool.wait_ge(sq_done, NB * (i + 1))
            nc.gpsimd.tensor_scalar(rstd[:, i], sumsq[:, i], 1.0 / D, EPS, ALU.mult, ALU.add).then_inc(rstd_chain, 1)
            pool.wait_ge(rstd_chain, i + 2)
            nc.gpsimd.tensor_tensor(rstd[:, i], rstd[:, i], half_power[:], ALU.pow).then_inc(rstd_done, 1)

        nc.gpsimd.memset(half_power[:], -0.5).then_inc(rstd_chain, 1)
        for i in range(3):
            rstds(i)
        pool.wait_ge(a_pv, HEADS)
        for n, g in enumerate((norm_ffn[1:2, :], final_norm.rearrange("(a n) -> a n", a=1))):
            pool.dma_start(mo["gain"][:, n], g.partition_broadcast(P).rearrange("p a n -> p (a n)")).then_inc(s_gain, 16)
        pool.dma_start(mo["rw"][:], router_w[0].rearrange("(k p) n -> p k n", p=P)).then_inc(s_rout, 16)
        pool.dma_start(mo["rb"][:], router_b[0:1, :].partition_broadcast(P).rearrange("p a n -> p (a n)")).then_inc(s_rout, 16)
        pool.dma_start(mo["before"][:], before_c).then_inc(s_rout, 16)
        pool.dma_start(mo["count"][:], count_c).then_inc(s_rout, 16)
        nc.gpsimd.memset(mo["ones"][:], 1.0).then_inc(ones_done, 1)
        nc.gpsimd.memset(mo["slot"][:], -1.0).then_inc(ones_done, 1)
        pool.wait_ge(s_gain, 32)
        for c in range(2):
            pool.wait_ge(h_half, 4 + c + 1)
            cs = slice(BANK * c, BANK * (c + 1))
            nc.gpsimd.tensor_tensor(hn[:, :, cs], h[:, :, cs], mo["gain"][:, 0:1, cs].to_broadcast([P, NB, BANK]),
                                    ALU.mult).then_inc(hn_done, 1)
        rstds(3)
        rstds(4)

    @block.scalar
    def _(act):
        made = [0]

        def split_hi(j, E):
            s, w = slot_of(j, E, RAW), slot_of(j, E, SPLIT)
            rounds = 16 * (j // RAW + 1) if E is None else 16 * ((N0 + j) // RAW + 1) + E * (16 * PER_EXPERT // RAW)
            act.wait_ge(raw_in[s], rounds)
            if has_before(j, E, SPLIT):
                act.wait_ge(piece_used, piece(j, E, SPLIT))
            nc.scalar.activation(w_hi[w][:], raw[s][:], ACT.Copy).then_inc(hi_made, 1)

        def split_past(n):
            while made[0] < min(n + SPLIT, N1):
                split_hi(made[0], None)
                made[0] += 1

        whole = [(s_x[1], 16), (h_half, 2), (h_half, 4), (h_half, 6), (moe_done, 1)]

        def squares(i):
            act.wait_ge(*whole[i])
            if i == 0:
                act.wait_ge(s_x[0], 16)
            for b in range(NB):
                terms = mo["hn_hi"] if i == 3 else hn
                nc.scalar.activation(terms[:, b], h[:, b], ACT.Square, accum_out=sumsq[:, i, b:b + 1]).then_inc(sq_done, 1)

        def stream_hi(i, half):
            for q in (2 * half, 2 * half + 1):
                act.wait_ge(tr_done, 4 * i + q + 1)
                for k in range(2):
                    last = nc.scalar.activation(act_hi[:, 2 * q + k], two(STREAM[i][q])[:, k], ACT.Copy,
                                                scale=gains[:, i, 2 * q + k:2 * q + k + 1])
                last.then_inc(act_hi_done, 1)

        act.dma_start(ident[:], ident_c).then_inc(s_const, 16)
        act.dma_start(gains[:], gains_c).then_inc(s_const, 16)
        act.dma_start(mask[:], mask_c).then_inc(s_mask, 16)
        act.wait_ge(s_const, 32)
        stream_hi(0, 0)
        stream_hi(0, 1)
        split_past(0)
        squares(0)
        act.wait_ge(rstd_done, 1)
        for c in range(2):
            split_past(at["w_in"][c][-1])
            for b in range(NB):
                projected(act, u_psum, c, at["w_in"][c], b)
                nc.scalar.activation(fo["u_hi"][:, b, BANK * c:BANK * (c + 1)], (G, U)[c][b][:], ACT.Copy,
                                     scale=rstd[:, 0, b:b + 1]).then_inc(u_hi_done, 1)
            if c == 0:
                act.wait_ge(s_dft, 16)
                nc.scalar.activation(fo["dft_hi"][:], fo["dft_raw"][:], ACT.Copy).then_inc(dft_hi_done, 1)
        for g in range(KD // 2 + 1):
            for m in (2 * g, 2 * g + 1) if g < KD // 2 else ():
                act.wait_ge(pt_psum, m + 1)
                if m >= PT:
                    act.wait_ge(ft_psum, m // 2 * 2 - PT + 2)
                nc.scalar.activation(fo["pt_hi"][:, m % PT], T[m % 2][:], ACT.Copy).then_inc(pt_hi_done, 1)
            for m in (2 * g - 2, 2 * g - 1) if g else ():
                act.wait_ge(ft_psum, m + 1)
                nc.scalar.activation(act_hi[:, m], Y[m % 2][:, :S], ACT.Copy).then_inc(ft_hi_done, 1)
        split_past(at["w_out"][0][-1] + 1)
        stream_hi(1, 0)
        split_past(at["w_out"][1][-1])
        stream_hi(1, 1)
        split_past(at["w_out"][1][-1] + 1)
        squares(1)
        def load_bias(step):
            half, rows = step // 2, HEADS * SHIFTS // 2
            r0 = rows * (step % 2)
            src = slide_c[half, r0:r0 + rows, 0:GRID]
            src = bass.AP(src.tensor, src.offset, [[1, GRID], [SLIDE, rows], [1, GRID]])
            act.dma_start(bias_raw[GRID * half:GRID * (half + 1), r0:r0 + rows], src).then_inc(s_bias[step], 16)

        def dense_hidden_hi(c):
            for b in range(NB):
                act.wait_ge(d_hidT, NB * c + b + 1)
                if c:
                    projected(act, d_down, c - 1, at["down"][c - 1], b)
                nc.scalar.activation(hidT_hi[b][:, :widths[c]], HT(c)[b][:, :widths[c]], ACT.Copy).then_inc(d_hidT_hi, 1)

        act.wait_ge(rstd_done, 2)
        for c in range(DC):
            w = widths[c]
            split_past(at["gate"][c][-1])
            for b in range(NB):
                projected(act, d_gate, c, at["gate"][c], b)
                if c:
                    act.wait_ge(d_hid, NB * (c - 1) + b + 1)
                nc.scalar.activation(silu_g[b][:, :w], G[b][:, :w], ACT.Silu, scale=rstd[:, 1, b:b + 1]).then_inc(d_silu, 1)
            if c:
                dense_hidden_hi(c - 1)
            split_past(at["up"][c][-1])
            if c < BIAS_STEPS:
                load_bias(c)
            if c:
                split_past(at["down"][c - 1][-1])
        dense_hidden_hi(DC - 1)
        split_past(at["down"][-1][-1])
        stream_hi(2, 0)
        stream_hi(2, 1)
        split_past(at["down"][-1][-1] + 1)
        squares(2)
        act.wait_ge(rstd_done, 3)
        act.wait_ge(bias_done, BIAS_STEPS)
        for c in range(6):
            split_past(at["qkv"][c][-1])
            projected(act, qkv_psum, c, at["qkv"][c], 0)
            if 2 <= c < 4:
                act.wait_ge(qkT_psum, 2 * (c - 1))
            dst = att["qk"][:, c % 2, 0] if c < 4 else att["v"][:, 0, BANK * (c - 4):BANK * (c - 3)]
            nc.scalar.activation(dst, (G, U)[c % 2][0][:], ACT.Copy, scale=rstd[:, 2, 0:1]).then_inc(qkv_act, 1)
            if 1 <= c < 5:
                act.wait_ge(qkT_psum, 2 * c - 1)
                dst = att["qT"] if c < 3 else att["kT"]
                m = 4 * ((c - 1) % 2)
                nc.scalar.activation(dst[:, m:m + 2], two((T, Y)[(c - 1) % 2][0]), ACT.Copy).then_inc(qT_act, 1)
        for i in range(HEADS + 2):
            if i < HEADS:
                act.wait_ge(a_max, i + 1)
                if i >= 2:
                    act.wait_ge(a_pT, i - 1)
                for b in range(NB):
                    last = nc.scalar.activation(hid[i % 2][:, S * b:S * (b + 1)], silu_g[i % 2][:, S * b:S * (b + 1)],
                                                ACT.Exp, bias=att["neg_max"][:, i % 2, b:b + 1],
                                                accum_out=att["p_sum"][:, NB - 1 - b, i:i + 1])
                    last.then_inc(a_exp, 1)
            if 2 <= i < HEADS + 2:
                g = i - 2
                act.wait_ge(a_pT, g + 1)
                if g >= 2:
                    act.wait_ge(a_pv, g - 1)
                nc.scalar.activation(att["probT"][:, g % 2], T[g % 2][:], ACT.Copy).then_inc(a_pTcopy, 1)
        for q in range(4):
            act.wait_ge(a_oT, q + 1)
            nc.scalar.activation(act_hi[:, 2 * q:2 * q + 2], two((G + T)[q]), ACT.Copy).then_inc(a_ohi, 1)
        split_past(at["wo"][0][-1] + 1)
        act.wait_ge(s_rout, 64)
        nc.scalar.activation(mo["rw_hi"][:], mo["rw"][:], ACT.Copy).then_inc(rw_hi_done, 1)
        stream_hi(3, 0)
        split_past(at["wo"][1][-1])
        stream_hi(3, 1)
        squares(3)
        act.wait_ge(rstd_done, 4)
        act.wait_ge(hn_done, 2)
        for b in range(NB):
            nc.scalar.activation(mo["hn_hi"][:, b], hn[:, b], ACT.Copy, scale=rstd[:, 3, b:b + 1]).then_inc(hnr_hi, 1)
        split_past(at["wo"][1][-1] + 1)
        act.wait_ge(gap_done, 1)
        nc.scalar.activation(mo["ratio"][:], mo["gap"][:], ACT.Exp).then_inc(ratio_done, 1)

        def gather_hi(E1):
            act.wait_ge(e_gather, E1)
            for q in range(2):
                last = nc.scalar.activation(mo["xg_hi"][:, 4 * q:4 * q + 4], four((G, U)[q][1]), ACT.Copy)
            last.then_inc(e_xhi, 1)

        def silu(E, c):
            act.wait_ge(piece_used, piece(AT["gate", c, 1], E))
            if c != 1:
                act.wait_ge(e_hid, E * STEPS + max(c - 1, 0))
            nc.scalar.activation(silu_g[c % 2][:], G[c % 2][:], ACT.Silu).then_inc(e_silu, 1)

        def hidden_hi(E, c):
            act.wait_ge(e_hidT, E * STEPS + (c + 1))
            if c != 1:
                act.wait_ge(piece_used, piece(AT["down", c - 2, 1] if c else -1, E))
            nc.scalar.activation(hidT_hi[c % 2][:], T[c % 2][:], ACT.Copy).then_inc(e_hidT_hi, 1)

        def result_hi(E):
            act.wait_ge(piece_used, piece(PER_EXPERT - 1, E))
            for q in range(2):
                last = nc.scalar.activation(mo["y_hi"][:, BANK * q:BANK * (q + 1)], Y[q][:], ACT.Copy)
            last.then_inc(e_yhi, 1)

        def expert(E, sweep):
            for j, (kind, c, half) in enumerate(EXPERT):
                if (kind, half) == ("gate", 1):
                    silu(E, c)
                    if c:
                        hidden_hi(E, c - 1)
                if (kind, c, half) == ("up", STEPS - 1, 1):
                    gather_hi(E + (sweep + 2))
                if (kind, c, half) == ("down", STEPS - 2, 0):
                    hidden_hi(E, STEPS - 1)
                if (kind, c, half) == ("down", STEPS - 1, 1):
                    result_hi(E)
                split_hi(j + SPLIT, E)

        gather_hi(1)
        with act.Fori(*EXPERTS[0]) as E:
            expert(E, 0)
        act.wait_ge(flag_done, 1)
        over = act.value_load(mo["flag"][0:1, 0:1], min_val=0, max_val=1)
        with act.If(over):
            gather_hi(NE + 2)
            with act.Fori(*EXPERTS[1]) as E:
                expert(E, 1)
        squares(4)

    @block.vector
    def _(dve):
        made = [0]
        chain = [0]

        def link(ins):
            chain[0] += 1
            ins.then_inc(dve_chain, 1)
            dve.wait_ge(dve_chain, chain[0])

        def split_lo(j, E):
            s, w = slot_of(j, E, RAW), slot_of(j, E, SPLIT)
            dve.wait_ge(hi_made, piece(j, E))
            nc.vector.tensor_tensor(w_lo[w][:], raw[s][:], w_hi[w][:].bitcast(f32), ALU.subtract).then_inc(lo_made, 1)

        def split_past(n):
            while made[0] < min(n + SPLIT, N1):
                split_lo(made[0], None)
                made[0] += 1

        def rest(out_, whole, hi):
            return nc.vector.tensor_tensor(out_, whole, hi.bitcast(f32), ALU.subtract)

        def rest_scaled(out_, whole, scale, hi):
            return nc.vector.scalar_tensor_tensor(out=out_, in0=whole, scalar=scale, in1=hi.bitcast(f32),
                                                  op0=ALU.mult, op1=ALU.subtract)

        def stream_lo(i, half):
            for q in (2 * half, 2 * half + 1):
                dve.wait_ge(act_hi_done, 4 * i + q + 1)
                for k in range(2):
                    kk = 2 * q + k
                    last = rest_scaled(act_lo[:, kk], two(STREAM[i][q])[:, k], gains[:, i, kk:kk + 1], act_hi[:, kk])
                last.then_inc(act_lo_done, 1)

        def add_projection(pieces, psum, i):
            for c in range(2):
                split_past(pieces[c][-1])
                for b in range(NB):
                    projected(dve, psum, c, pieces[c], b)
                    part = h[:, b, BANK * c:BANK * (c + 1)]
                    last = nc.vector.tensor_tensor(part, (G, U)[c][b][:], part, ALU.add)
                last.then_inc(h_half, 1)
                if c == 0:
                    split_past(pieces[0][-1] + 1)
                stream_lo(i, c)
            split_past(pieces[-1][-1] + 1)

        def mask_bias(step):
            half, rows = step // 2, HEADS * SHIFTS // 2
            p0, r0 = GRID * half, rows * (step % 2)
            dve.wait_ge(s_bias[step], 16)
            if step == 0:
                dve.wait_ge(s_mask, 16)
            full = [GRID, rows, GRID]
            a = bias_raw[p0:p0 + GRID, r0:r0 + rows]
            back = bass.AP(a.tensor, a.offset + GRID - 1, [a.ap[0], [GRID, rows], [-1, GRID]])
            nc.vector.tensor_tensor(fo["bias"][p0:p0 + GRID, r0:r0 + rows], back,
                                    mask[p0:p0 + GRID].unsqueeze(1).to_broadcast(full), ALU.add).then_inc(bias_done, 1)

        dve.wait_ge(s_const, 32)
        stream_lo(0, 0)
        stream_lo(0, 1)
        split_past(0)
        dve.wait_ge(rstd_done, 1)
        for c in range(2):
            split_past(at["w_in"][c][-1])
            for b in range(NB):
                dve.wait_ge(u_hi_done, NB * c + b + 1)
                cs = slice(BANK * c, BANK * (c + 1))
                rest_scaled(fo["u_lo"][:, b, cs], (G, U)[c][b][:], rstd[:, 0, b:b + 1], fo["u_hi"][:, b, cs]).then_inc(u_lo_done, 1)
            if c == 0:
                dve.wait_ge(dft_hi_done, 1)
                rest(fo["dft_lo"][:], fo["dft_raw"][:], fo["dft_hi"][:]).then_inc(dft_lo_done, 1)
        for g in range(KD // 2 + 1):
            for m in (2 * g, 2 * g + 1) if g < KD // 2 else ():
                dve.wait_ge(pt_hi_done, m + 1)
                rest(fo["pt_lo"][:, m % PT], T[m % 2][:], fo["pt_hi"][:, m % PT]).then_inc(pt_lo_done, 1)
            for m in (2 * g - 2, 2 * g - 1) if g else ():
                dve.wait_ge(ft_hi_done, m + 1)
                rest(act_lo[:, m], Y[m % 2][:, :S], act_hi[:, m]).then_inc(ft_lo_done, 1)
        add_projection(at["w_out"], fo_psum, 1)

        def hidden_lo(c):
            for b in range(NB):
                dve.wait_ge(d_hidT_hi, NB * c + b + 1)
                rest(hidT_lo[b][:, :widths[c]], HT(c)[b][:, :widths[c]], hidT_hi[b][:, :widths[c]]).then_inc(d_hidT_lo, 1)

        def add_down(c):
            for b in range(NB):
                projected(dve, d_down, c, at["down"][c], b)
                for q in range(2):
                    part = h[:, b, BANK * q:BANK * (q + 1)]
                    last = nc.vector.tensor_tensor(part, (Y, T)[b][q][:], part, ALU.add)
                last.then_inc(d_added, 1)

        dve.wait_ge(rstd_done, 2)
        for c in range(DC):
            w = widths[c]
            split_past(at["gate"][c][-1])
            if c:
                hidden_lo(c - 1)
            split_past(at["up"][c][-1])
            for b in range(NB):
                dve.wait_ge(d_silu, NB * c + b + 1)
                projected(dve, d_up, c, at["up"][c], b)
                if c:
                    dve.wait_ge(d_hidT, NB * (c - 1) + b + 1)
                nc.vector.scalar_tensor_tensor(out=hid[b][:, :w], in0=U[b][:, :w], scalar=rstd[:, 1, b:b + 1],
                                               in1=silu_g[b][:, :w], op0=ALU.mult, op1=ALU.mult).then_inc(d_hid, 1)
            if c:
                split_past(at["down"][c - 1][-1])
                add_down(c - 1)
                if c <= BIAS_STEPS:
                    mask_bias(c - 1)
        hidden_lo(DC - 1)
        split_past(at["down"][-1][-1])
        for q in range(2):
            projected(dve, d_down, DC - 1, at["down"][-1], q)
            for b in range(NB):
                part = h[:, b, BANK * q:BANK * (q + 1)]
                last = nc.vector.tensor_tensor(part, (Y, T)[b][q][:], part, ALU.add)
            last.then_inc(h_half, 1)
            stream_lo(2, q)
        split_past(at["down"][-1][-1] + 1)
        dve.wait_ge(rstd_done, 3)
        for c in range(6):
            split_past(at["qkv"][c][-1])
            projected(dve, qkv_psum, c, at["qkv"][c], 1)
            if 2 <= c < 4:
                dve.wait_ge(qkT_psum, 2 * (c - 1))
            dst = att["qk"][:, c % 2, 1] if c < 4 else att["v"][:, 1, BANK * (c - 4):BANK * (c - 3)]
            nc.vector.tensor_scalar(dst, (G, U)[c % 2][1][:], rstd[:, 2, 1:2], None, ALU.mult).then_inc(qkv_dve, 1)
            if 1 <= c < 5:
                dve.wait_ge(qkT_psum, 2 * c)
                dst = att["qT"] if c < 3 else att["kT"]
                m = 4 * ((c - 1) % 2)
                nc.vector.tensor_copy(dst[:, m + 2:m + 4], two((T, Y)[(c - 1) % 2][1])).then_inc(qT_dve, 1)
        def head_bias(i):
            a = att["bias"][:, SHIFTS * i:SHIFTS * (i + 1)]
            return bass.AP(a.tensor, a.offset, [a.ap[0], [(ROWS - 2) * GRID, NB], [1, S]])

        dve.wait_ge(bias_done, BIAS_STEPS)
        def outputs(hg):
            hs = slice(HEADS // 2 * hg, HEADS // 2 * (hg + 1))
            dve.wait_ge(a_exp, NB * HEADS // 2 * (hg + 1))
            nc.vector.reciprocal(att["p_inv"][:, :, hs], att["p_sum"][:, :, hs]).then_inc(a_inv, 1)
            dve.wait_ge(a_inv, hg + 1)
            dve.wait_ge(a_pv, HEADS // 2 * (hg + 1))
            for b in range(NB):
                last = nc.vector.tensor_tensor(hn[:, b, BANK * hg:BANK * (hg + 1)].rearrange("p (h d) -> p h d", d=HD),
                                               OB[b][hg][:].rearrange("p (h d) -> p h d", d=HD),
                                               att["p_inv"][:, b, hs].unsqueeze(2).to_broadcast([P, HEADS // 2, HD]), ALU.mult)
            last.then_inc(a_out, 1)

        for i in range(HEADS):
            if i == HEADS // 2 + 4:
                outputs(0)
            if i < HEADS:
                dve.wait_ge(a_score, i + 1)
                if i >= 2:
                    dve.wait_ge(a_exp, NB * (i - 1))
                nc.vector.scalar_tensor_tensor(out=silu_g[i % 2][:].rearrange("p (n k) -> p n k", n=NB), in0=two(G[i % 2]), scalar=float(HD) ** -0.5,
                                               in1=head_bias(i), op0=ALU.mult,
                                               op1=ALU.add).then_inc(a_biased, 1)
                dve.wait_ge(a_biased, i + 1)
                nc.vector.tensor_reduce(att["neg_max"][:, i % 2], silu_g[i % 2][:].rearrange("p (b k) -> p b k", b=NB),
                                        AX.X, ALU.max, negate=True).then_inc(a_max, 1)
        outputs(1)
        for q in range(4):
            dve.wait_ge(a_ohi, q + 1)
            rest(act_lo[:, 2 * q:2 * q + 2], two((G + T)[q]), act_hi[:, 2 * q:2 * q + 2]).then_inc(a_olo, 1)
        dve.wait_ge(rw_hi_done, 1)
        rest(mo["rw_lo"][:], mo["rw"][:], mo["rw_hi"][:]).then_inc(rw_lo_done, 1)
        add_projection(at["wo"], ao_psum, 3)

        dve.wait_ge(rstd_done, 4)
        dve.wait_ge(logit_psum, 1)
        full = [P, NB, NE]

        def each_token(t):
            return t.unsqueeze(2).to_broadcast(full)

        iota = mo["count"][:, 0:NE].unsqueeze(1).to_broadcast(full)
        for b in range(NB):
            link(nc.vector.scalar_tensor_tensor(out=mo["logit"][:, b], in0=G[0][:, NE * b:NE * (b + 1)], scalar=rstd[:, 3, b:b + 1],
                                                in1=mo["rb"][:], op0=ALU.mult, op1=ALU.add))
        for n, (src, one) in enumerate((("logit", "first"), ("rest", "second"))):
            link(nc.vector.tensor_reduce(mo["top"][:, n], mo[src][:], AX.X, ALU.max))
            link(nc.vector.tensor_tensor(mo["eq"][:], mo[src][:], each_token(mo["top"][:, n]), ALU.is_equal))
            link(nc.vector.scalar_tensor_tensor(out=mo["cand"][:], in0=iota, scalar=-float(NE), in1=mo["eq"][:],
                                                op0=ALU.add, op1=ALU.mult))
            link(nc.vector.tensor_reduce(mo["idx"][:, n], mo["cand"][:], AX.X, ALU.min))
            link(nc.vector.tensor_scalar(mo["idx"][:, n], mo["idx"][:, n], float(NE), None, ALU.add))
            link(nc.vector.tensor_tensor(mo[one][:], iota, each_token(mo["idx"][:, n]), ALU.is_equal))
            if n == 0:
                link(nc.vector.scalar_tensor_tensor(out=mo["rest"][:], in0=mo["first"][:], scalar=-3e38,
                                                    in1=mo["logit"][:], op0=ALU.mult, op1=ALU.add))
        nc.vector.tensor_tensor(mo["used"][:], mo["first"][:], mo["second"][:], ALU.add).then_inc(used_done, 1)
        nc.vector.tensor_tensor(mo["gap"][:], mo["top"][:, 1], mo["top"][:, 0], ALU.subtract).then_inc(gap_done, 1)
        dve.wait_ge(used_done, 1)
        dve.wait_ge(rank_psum, 1)
        dve.wait_ge(ones_done, 2)
        slots = mo["slot"][:, :, 0:NE]
        link(nc.vector.scalar_tensor_tensor(out=slots, in0=G[1][:, 0:NB * NE].rearrange("p (b e) -> p b e", b=NB),
                                            scalar=1.0, in1=mo["used"][:], op0=ALU.add, op1=ALU.mult))
        link(nc.vector.tensor_scalar(slots, slots, -1.0, None, ALU.add))
        link(nc.vector.tensor_reduce(mo["most"][:], G[1][:, NB * NE:(NB + 1) * NE], AX.X, ALU.max))
        nc.vector.tensor_scalar(mo["flag"][:], mo["most"][:], float(P), None, ALU.is_gt).then_inc(flag_done, 1)

        def select(sweep, e):
            for b in range(NB):
                last = nc.vector.tensor_scalar(mo["sel"][:, b], mo["count"][:, P * sweep:P * (sweep + 1)],
                                               mo["slot"][:, b, bass.ds(e, 1)], None, ALU.is_equal)
            last.then_inc(e_sel, 1)

        def gather_lo(E1):
            dve.wait_ge(e_xhi, E1)
            for q in range(2):
                last = rest(mo["xg_lo"][:, 4 * q:4 * q + 4], four((G, U)[q][1]),
                            mo["xg_hi"][:, 4 * q:4 * q + 4])
            last.then_inc(e_xlo, 1)

        def hidden(E, c):
            dve.wait_ge(e_silu, E * STEPS + (c + 1))
            dve.wait_ge(piece_used, piece(AT["up", c, 1], E))
            if c != 1:
                dve.wait_ge(e_hidT, E * STEPS + max(c - 1, 0))
            nc.vector.tensor_tensor(hid[c % 2][:], U[c % 2][:], silu_g[c % 2][:], ALU.mult).then_inc(e_hid, 1)

        def hidden_rest(E, c):
            dve.wait_ge(e_hidT_hi, E * STEPS + (c + 1))
            rest(hidT_lo[c % 2][:], T[c % 2][:], hidT_hi[c % 2][:]).then_inc(e_hidT_lo, 1)

        def next_selection(E, e, sweep):
            dve.wait_ge(e_selT, E + 1)
            dve.wait_ge(e_scatter, E)
            nc.vector.tensor_copy(mo["selT"][:], T[1][:, :NB * P].rearrange("p (b t) -> p b t", b=NB)).then_inc(e_selT_copy, 1)
            select(sweep, e + 1)

        def result_rest(E):
            dve.wait_ge(e_yhi, E + 1)
            for q in range(2):
                cs = slice(BANK * q, BANK * (q + 1))
                last = rest(mo["y_lo"][:, cs], Y[q][:], mo["y_hi"][:, cs])
            last.then_inc(e_ylo, 1)

        def add_result(E, e):
            dve.wait_ge(e_scatter, E + 1)
            for b in range(NB):
                for q in range(2):
                    part = h[:, b, BANK * q:BANK * (q + 1)]
                    src = T[q] if b == 0 else (G, U)[q][1]
                    last = nc.vector.scalar_tensor_tensor(out=part, in0=src[:], scalar=mo["weight"][:, b, bass.ds(e, 1)],
                                                          in1=part, op0=ALU.mult, op1=ALU.add)
            last.then_inc(e_added, 1)

        def expert(E, sweep):
            e = E - NE if sweep else E
            for j, (kind, c, half) in enumerate(EXPERT):
                if (kind, c, half) == ("gate", 0, 1):
                    next_selection(E, e, sweep)
                elif (kind, half) == ("gate", 1):
                    hidden_rest(E, c - 1)
                if (kind, half) == ("up", 1):
                    hidden(E, c)
                    if c == STEPS - 1:
                        gather_lo(E + (sweep + 2))
                if (kind, c, half) == ("down", STEPS - 2, 0):
                    hidden_rest(E, STEPS - 1)
                if (kind, c, half) == ("down", STEPS - 1, 1):
                    result_rest(E)
                    add_result(E, e)
                split_lo(j + SPLIT, E)

        select(0, 0)
        for b in range(NB):
            dve.wait_ge(hnr_hi, b + 1)
            rest_scaled(mo["hn_lo"][:, b], hn[:, b], rstd[:, 3, b:b + 1], mo["hn_hi"][:, b]).then_inc(hnr_lo, 1)
        dve.wait_ge(ratio_done, 1)
        link(nc.vector.tensor_scalar(mo["den"][:], mo["ratio"][:], 1.0, None, ALU.add))
        link(nc.vector.reciprocal(mo["g1"][:], mo["den"][:]))
        link(nc.vector.tensor_tensor(mo["g2"][:], mo["ratio"][:], mo["g1"][:], ALU.mult))
        link(nc.vector.tensor_tensor(mo["first"][:], mo["first"][:], each_token(mo["g1"][:]), ALU.mult))
        link(nc.vector.tensor_tensor(mo["second"][:], mo["second"][:], each_token(mo["g2"][:]), ALU.mult))
        link(nc.vector.tensor_tensor(mo["weight"][:], mo["first"][:], mo["second"][:], ALU.add))
        gather_lo(1)
        with dve.Fori(*EXPERTS[0]) as E:
            expert(E, 0)
        dve.wait_ge(flag_done, 1)
        over = dve.value_load(mo["flag"][0:1, 0:1], min_val=0, max_val=1)
        with dve.If(over):
            dve.wait_ge(e_gather, NE + 1)
            select(1, 0)
            gather_lo(NE + 2)
            with dve.Fori(*EXPERTS[1]) as E:
                expert(E, 1)
            dve.wait_ge(e_added, 2 * NE)
        dve.wait_ge(e_added, NE)
        dve.sem_inc(moe_done, 1)
        dve.wait_ge(rstd_done, 5)
        dve.wait_ge(s_gain, 32)
        for b in range(NB):
            nc.vector.scalar_tensor_tensor(out=hn[:, b], in0=h[:, b], scalar=rstd[:, 4, b:b + 1], in1=mo["gain"][:, 1],
                                           op0=ALU.mult, op1=ALU.mult).then_inc(fin_done, 1)

    @block.tensor
    def _(pe):
        def ready(j, E):
            pe.wait_ge(lo_made, piece(j, E))

        def parts(j, E, tiles):
            w = slot_of(j, E, SPLIT)
            return [t[:].rearrange("p (k n) -> p k n", k=tiles) for t in (w_hi[w], w_lo[w])]

        def three(out_, xh, xl, wh, wl, start, stop):
            nc.tensor.matmul(out_, xh, wh, start=start, stop=False)
            nc.tensor.matmul(out_, xh, wl, start=False, stop=False)
            return nc.tensor.matmul(out_, xl, wh, start=False, stop=stop)

        def project(pieces, banks, width, done, before=lambda n, b: None):
            for n, j in enumerate(pieces):
                tiles = PIECE // width
                ready(j, None)
                wh, wl = parts(j, None, tiles)
                for b in range(NB):
                    before(n, b)
                    for k in range(tiles):
                        kk = tiles * n + k
                        last = three(banks[b][:, :width], act_hi[:, kk, P * b:P * (b + 1)], act_lo[:, kk, P * b:P * (b + 1)],
                                     wh[:, k], wl[:, k], kk == 0, kk == KD - 1)
                    if n == len(pieces) - 1 and b < NB - 1:
                        last.then_inc(done, 1)
                last.then_inc(piece_used, 1)

        def transpose_stream(i, half):
            if i == 0:
                pe.wait_ge(s_x[half], 16)
            else:
                pe.wait_ge(h_half, 2 * (i - 1) + half + 1)
            for q in (2 * half, 2 * half + 1):
                for k in range(2):
                    for b in range(NB):
                        o = S * k + P * b
                        kk = 2 * q + k
                        last = nc.tensor.transpose(STREAM[i][q][:, o:o + P], h[:, b, P * kk:P * (kk + 1)], ident[:])
                last.then_inc(tr_done, 1)

        def stream_first(i):
            def before(n, b):
                if (n, b) == (1, 0):
                    transpose_stream(i, 0)
            return before

        def stream_second(i):
            def before(n, b):
                if (n, b) == (0, 0):
                    pe.wait_ge(act_lo_done, 4 * i + 2)
                if (n, b) == (0, 1) and i > 0:
                    transpose_stream(i, 1)
                if (n, b) == (1, 0):
                    pe.wait_ge(act_lo_done, 4 * i + 4)
            return before

        pe.wait_ge(s_const, 32)
        transpose_stream(0, 0)
        transpose_stream(0, 1)
        project(at["w_in"][0], G, BANK, u_psum, stream_second(0))
        project(at["w_in"][1], U, BANK, u_psum)
        pe.wait_ge(dft_lo_done, 1)
        def token_dft(m):
            if m == 0:
                pe.wait_ge(u_lo_done, NB)
            if m == KD // 2:
                pe.wait_ge(u_lo_done, 2 * NB)
            if m >= 2:
                pe.wait_ge(pt_lo_done, m - 1)
            for b in range(NB):
                last = three(T[m % 2][:], fo["u_hi"][:, b, P * m:P * (m + 1)], fo["u_lo"][:, b, P * m:P * (m + 1)],
                             fo["dft_hi"][:, b, 0:2 * S], fo["dft_lo"][:, b, 0:2 * S], b == 0, b == NB - 1)
            last.then_inc(pt_psum, 1)

        def channel_dft(m):
            g0 = m // 2 * 2
            pe.wait_ge(pt_lo_done, g0 + 2)
            if m >= 2:
                pe.wait_ge(ft_lo_done, m - 1)
            terms = [(k, part) for k in range(2) for part in range(2)]
            for n, (k, part) in enumerate(terms):
                o = (0, 2 * S)[part] + P * (m % 2)
                last = three(Y[m % 2][:, :S], fo["dft_hi"][:, k, o:o + P], fo["dft_lo"][:, k, o:o + P],
                             fo["pt_hi"][:, (g0 + k) % PT, S * part:S * (part + 1)],
                             fo["pt_lo"][:, (g0 + k) % PT, S * part:S * (part + 1)], n == 0, n == len(terms) - 1)
            last.then_inc(ft_psum, 1)

        for g in range(KD // 2 + 1):
            for m in (2 * g, 2 * g + 1) if g < KD // 2 else ():
                token_dft(m)
            for m in (2 * g - 2, 2 * g - 1) if g else ():
                channel_dft(m)
        pe.wait_ge(ft_lo_done, KD)
        project(at["w_out"][0], G, BANK, fo_psum)
        project(at["w_out"][1], U, BANK, fo_psum, stream_first(1))


        def hidden_transposes(c):
            for b in range(NB):
                pe.wait_ge(d_hid, NB * c + b + 1)
                if c and c < DC - 1:
                    pe.wait_ge(d_added, NB * c)
                for k in range(widths[c] // P):
                    last = nc.tensor.transpose(HT(c)[b][:, P * k:P * (k + 1)], hid[b][:, P * k:P * (k + 1)], ident[:])
                last.then_inc(d_hidT, 1)

        def down(c, between=lambda: None):
            pieces = at["down"][c]
            for j in pieces:
                ready(j, None)
            pe.wait_ge(d_hidT_lo, NB * (c + 1))
            for b in range(NB):
                if b:
                    between()
                if c:
                    pe.wait_ge(d_added, NB * (c - 1) + b + 1)
                for n, j in enumerate(pieces):
                    wh, wl = parts(j, None, KROW)
                    for k in range(KROW):
                        kk = KROW * n + k
                        for q in range(2):
                            cs = slice(BANK * q, BANK * (q + 1))
                            last = three((Y, T)[b][q][:], hidT_hi[b][:, P * kk:P * (kk + 1)], hidT_lo[b][:, P * kk:P * (kk + 1)],
                                         wh[:, k, cs], wl[:, k, cs], kk == 0, kk == KROW * len(pieces) - 1)
                    if b == NB - 1:
                        last.then_inc(piece_used, 1)
                if b < NB - 1:
                    last.then_inc(d_down, 1)

        def last_down():
            (j,) = at["down"][DC - 1]
            ready(j, None)
            pe.wait_ge(d_hidT_lo, NB * DC)
            pe.wait_ge(d_added, NB * (DC - 1))
            wh, wl = parts(j, None, KROW)
            for q in range(2):
                for b in range(NB):
                    if (q, b) == (1, 1):
                        transpose_stream(2, 0)
                    for k in range(KROW):
                        last = three((Y, T)[b][q][:], hidT_hi[b][:, P * k:P * (k + 1)], hidT_lo[b][:, P * k:P * (k + 1)],
                                     wh[:, k, BANK * q:BANK * (q + 1)], wl[:, k, BANK * q:BANK * (q + 1)], k == 0, k == KROW - 1)
                last.then_inc((d_down, piece_used)[q], 1)

        for c in range(DC):
            if c == 0:
                project(at["gate"][0], G, widths[0], d_gate, stream_second(1))
            else:
                pe.wait_ge(d_silu, NB * c)
                project(at["gate"][c], G, widths[c], d_gate)
                hidden_transposes(c - 1)
                pe.wait_ge(d_hid, NB * c)
            project(at["up"][c], U, widths[c], d_up)
            if 0 < c < DC - 1:
                down(c - 1)
        down(DC - 2, lambda: hidden_transposes(DC - 1))
        last_down()


        def transpose_qk(c):
            pe.wait_ge(qkv_act, c + 1)
            pe.wait_ge(qkv_dve, c + 1)
            if c >= 2:
                pe.wait_ge(qT_act, c - 1)
                pe.wait_ge(qT_dve, c - 1)
            for t in range(2):
                for k in range(2):
                    for b in range(NB):
                        o = S * k + P * b
                        m = 2 * t + k
                        last = nc.tensor.transpose((T, Y)[c % 2][t][:, o:o + P], att["qk"][:, c % 2, b, P * m:P * (m + 1)], ident[:])
                last.then_inc(qkT_psum, 1)

        for c in range(6):
            if c >= 2:
                pe.wait_ge(qkv_act, c - 1)
                pe.wait_ge(qkv_dve, c - 1)
            project(at["qkv"][c], (G, U)[c % 2], BANK, qkv_psum, stream_second(2) if c == 0 else lambda n, b: None)
            if 1 <= c < 5:
                transpose_qk(c - 1)
        pe.wait_ge(qkv_act, 6)
        pe.wait_ge(qkv_dve, 6)
        pe.wait_ge(qT_act, 4)
        pe.wait_ge(qT_dve, 4)
        for i in range(HEADS + 3):
            if i < HEADS:
                m, p0 = i // 2, HD * (i % 2)
                if i >= 2:
                    pe.wait_ge(a_biased, i - 1)
                for b in range(NB):
                    n = NB - 1 - b
                    last = nc.tensor.matmul(G[i % 2][:, S * n:S * (n + 1)], att["qT"][p0:p0 + HD, m, P * b:P * (b + 1)],
                                            att["kT"][p0:p0 + HD, m, :], start=True, stop=True)
                last.then_inc(a_score, 1)
            if 2 <= i < HEADS + 2:
                g = i - 2
                pe.wait_ge(a_exp, NB * (g + 1))
                if g >= 2:
                    pe.wait_ge(a_pTcopy, g - 1)
                for k in range(NB):
                    for b in range(NB):
                        o, n = S * k + P * b, NB - 1 - b
                        last = nc.tensor.transpose(T[g % 2][:, o:o + P], hid[g % 2][:, S * n + P * k:S * n + P * (k + 1)], ident[:])
                last.then_inc(a_pT, 1)
            if i >= 3:
                g = i - 3
                pe.wait_ge(a_pTcopy, g + 1)
                o = HD * (g % (HEADS // 2))
                for b in range(NB):
                    for k in range(NB):
                        last = nc.tensor.matmul(OB[b][g // (HEADS // 2)][:, o:o + HD], att["probT"][:, g % 2, S * k + P * b:S * k + P * (b + 1)],
                                                att["v"][:, k, HD * g:HD * (g + 1)], start=(k == 0), stop=(k == NB - 1))
                last.then_inc(a_pv, 1)
        for q in range(4):
            pe.wait_ge(a_out, q // 2 + 1)
            for k in range(2):
                for b in range(NB):
                    o, kk = S * k + P * b, 2 * q + k
                    last = nc.tensor.transpose((G + T)[q][:, o:o + P], hn[:, b, P * kk:P * (kk + 1)], ident[:])
            last.then_inc(a_oT, 1)
        pe.wait_ge(a_olo, 4)
        project(at["wo"][0], G, BANK, ao_psum)
        project(at["wo"][1], U, BANK, ao_psum, stream_first(3))

        transpose_stream(3, 1)
        pe.wait_ge(rw_lo_done, 1)
        pe.wait_ge(act_lo_done, 4 * 3 + 4)
        for b in range(NB):
            for k in range(KD):
                last = three(G[0][:, NE * b:NE * (b + 1)], act_hi[:, k, P * b:P * (b + 1)], act_lo[:, k, P * b:P * (b + 1)],
                             mo["rw_hi"][:, k], mo["rw_lo"][:, k], k == 0, k == KD - 1)
        last.then_inc(logit_psum, 1)
        pe.wait_ge(used_done, 1)
        pe.wait_ge(ones_done, 2)
        pe.wait_ge(s_rout, 64)
        used = mo["used"]
        nc.tensor.matmul(G[1][:, 0:NE], mo["before"][:], used[:, 0], start=True, stop=True)
        nc.tensor.matmul(G[1][:, NE:2 * NE], mo["ones"][:], used[:, 0], start=True, stop=False)
        nc.tensor.matmul(G[1][:, NE:2 * NE], mo["before"][:], used[:, 1], start=False, stop=True)
        nc.tensor.matmul(G[1][:, 2 * NE:3 * NE], mo["ones"][:], used[:, 0], start=True, stop=False)
        nc.tensor.matmul(G[1][:, 2 * NE:3 * NE], mo["ones"][:], used[:, 1], start=False, stop=True).then_inc(rank_psum, 1)

        def gather():
            for k in range(KD):
                o = (G, U)[k // 4][1][:, P * (k % 4):P * (k % 4 + 1)]
                for n, (b, part) in enumerate([(b, part) for b in range(NB) for part in ("hn_hi", "hn_lo")]):
                    last = nc.tensor.matmul(o, mo[part][:, b, P * k:P * (k + 1)], mo["sel"][:, b], start=(n == 0), stop=(n == 3))
            last.then_inc(e_gather, 1)

        def expert(E, sweep):
            def columns(kind, c, bk):
                for half in range(2):
                    j = AT[kind, c, half]
                    ready(j, E)
                    wh, wl = parts(j, E, KH)
                    for k in range(KH):
                        kk = KH * half + k
                        last = three(bk[:], mo["xg_hi"][:, kk], mo["xg_lo"][:, kk], wh[:, k], wl[:, k], kk == 0, kk == KD - 1)
                    last.then_inc(piece_used, 1)

            def hidden_transposes(c):
                pe.wait_ge(e_hid, E * STEPS + (c + 1))
                if c >= 2:
                    pe.wait_ge(e_hidT_lo, E * STEPS + (c - 1))
                if c == 1:
                    pe.wait_ge(e_selT_copy, E + 1)
                for k in range(BANK // P):
                    last = nc.tensor.transpose(T[c % 2][:, P * k:P * (k + 1)], hid[c % 2][:, P * k:P * (k + 1)], ident[:])
                last.then_inc(e_hidT, 1)

            def down(c, half):
                j = AT["down", c, half]
                ready(j, E)
                if half == 0:
                    pe.wait_ge(e_hidT_lo, E * STEPS + (c + 1))
                    if c == 0:
                        pe.wait_ge(e_ylo, E)
                wh, wl = parts(j, E, KROW)
                for k in range(KROW):
                    kk = KROW * half + k
                    for q in range(2):
                        cs = slice(BANK * q, BANK * (q + 1))
                        last = three(Y[q][:], hidT_hi[c % 2][:, P * kk:P * (kk + 1)], hidT_lo[c % 2][:, P * kk:P * (kk + 1)],
                                     wh[:, k, cs], wl[:, k, cs], c == 0 and kk == 0, c == STEPS - 1 and kk == BANK // P - 1)
                last.then_inc(piece_used, 1)

            for c in range(STEPS):
                if c == 0:
                    pe.wait_ge(e_xlo, E + (sweep + 1))
                    pe.wait_ge(e_silu, E * STEPS)
                elif c == 1:
                    pe.wait_ge(e_added, E)
                else:
                    pe.wait_ge(e_silu, E * STEPS + (c - 1))
                columns("gate", c, G[c % 2])
                if c == 0:
                    pe.wait_ge(e_added, E)
                    pe.wait_ge(e_sel, E + (sweep + 1))
                    for b in range(NB):
                        last = nc.tensor.transpose(T[1][:, P * b:P * (b + 1)], mo["sel"][:, b].bitcast(f32), ident[:])
                    last.then_inc(e_selT, 1)
                else:
                    hidden_transposes(c - 1)
                if c != 1:
                    pe.wait_ge(e_hid, E * STEPS + max(c - 1, 0))
                columns("up", c, U[c % 2])
                if 1 <= c < STEPS - 1:
                    down(c - 1, 0)
                    down(c - 1, 1)
            pe.wait_ge(e_sel, E + (sweep + 2))
            pe.wait_ge(e_hid, E * STEPS + (STEPS - 1))
            gather()
            down(STEPS - 2, 0)
            hidden_transposes(STEPS - 1)
            down(STEPS - 2, 1)
            down(STEPS - 1, 0)
            down(STEPS - 1, 1)
            pe.wait_ge(e_ylo, E + 1)
            pe.wait_ge(e_selT_copy, E + 1)
            pe.wait_ge(e_xlo, E + (sweep + 2))
            for b in range(NB):
                for q in range(2):
                    cs = slice(BANK * q, BANK * (q + 1))
                    bk = T[q] if b == 0 else (G, U)[q][1]
                    nc.tensor.matmul(bk[:], mo["selT"][:, b], mo["y_hi"][:, cs], start=True, stop=False)
                    last = nc.tensor.matmul(bk[:], mo["selT"][:, b], mo["y_lo"][:, cs], start=False, stop=True)
            last.then_inc(e_scatter, 1)

        pe.wait_ge(hnr_lo, NB)
        pe.wait_ge(e_sel, 1)
        gather()
        with pe.Fori(*EXPERTS[0]) as E:
            expert(E, 0)
        pe.wait_ge(flag_done, 1)
        over = pe.value_load(mo["flag"][0:1, 0:1], min_val=0, max_val=1)
        with pe.If(over):
            pe.wait_ge(e_added, NE)
            pe.wait_ge(e_sel, NE + 2)
            gather()
            with pe.Fori(*EXPERTS[1]) as E:
                expert(E, 1)

    block.__exit__(None, None, None)


_INS = ["x", "norm_mix", "norm_ffn", "fourier_w_in", "fourier_w_out", "nat_w_qkv", "nat_w_o",
        "ffn_w_gate", "ffn_w_up", "ffn_w_down", "router_w", "router_b", "expert_w_gate", "expert_w_up",
        "expert_w_down", "final_norm"]
_OUTS = [((1, S, D), "float32")]


def shape_constants():
    turn = 2 * np.pi * (np.outer(np.arange(S), np.arange(S)) % S) / S
    cos, sin = np.cos(turn) / np.sqrt(S), np.sin(turn) / np.sqrt(S)
    dft = np.concatenate([cos, sin, -sin], 1).astype(np.float32)
    q, k = np.arange(P)[:, None] % GRID, np.arange(GRID)[None, :]
    start = np.clip(q - WIN_W // 2, 0, GRID - WIN_W)
    mask = np.where((k >= start) & (k < start + WIN_W), 0.0, MASKED).astype(np.float32)
    before = np.triu(np.ones((P, P), np.float32), 1)
    count = np.tile(np.arange(S, dtype=np.float32), (P, 1))
    return {"dft": dft, "mask": mask, "ident": np.eye(P, dtype=np.float32), "before": before, "count": count}


def kernel(**inputs):
    import concourse.bacc as bacc
    from concourse.bass_utils import run_bass_kernel_spmd

    nc = bacc.Bacc("TRN2", target_bir_lowering=False, num_devices=1, dynamic_dma_scratch_size=8192)
    arrays, args = {}, []
    slide = np.zeros((2, HEADS, SHIFTS, SLIDE), np.float32)
    for half in range(2):
        d0 = WIN_H_MAX - 1 - (ROWS - 2) - half
        slide[half, :, :, GRID - WIN_W:GRID - WIN_W + RPB_W] = inputs["nat_rpb"][0][:, d0:d0 + SHIFTS, ::-1]
    slide = slide.reshape(2, HEADS * SHIFTS, SLIDE)
    gains = np.stack([inputs["norm_mix"], inputs["norm_ffn"]], 1).reshape(4, KD, P).transpose(2, 0, 1)
    for name, a in [(n, inputs[n]) for n in _INS] + [("gains", gains), ("slide", slide)] + list(shape_constants().items()):
        a = np.ascontiguousarray(a)
        arrays[f"in_{name}"] = a
        args.append(nc.dram_tensor(f"in_{name}", a.shape, mybir.dt.from_np(a.dtype), kind="ExternalInput").ap())
    for i, (shape, dtype) in enumerate(_OUTS):
        args.append(nc.dram_tensor(f"out_{i}", shape, mybir.dt.from_np(np.dtype(dtype)), kind="ExternalOutput").ap())
    trunk(nc, *args)
    r = run_bass_kernel_spmd(nc, [arrays], core_ids=[0])
    return r.results[0]["out_0"]
```

```python
import concourse.bass as bass
from concourse import mybir
import numpy as np

P = 128
D = 1024
S = 256
NB = S // P
KD = D // P
GRID = 64
ROWS = S // GRID
WIN_W = 16
WIN_H_MAX = 8
HEADS = 16
HD = D // HEADS
FF = 2816
FFE = 3584
NE = 8
EPS = 1e-6
BANK = 512
PIECE = 2048
RAW = 7
SPLIT = 3
KH = PIECE // BANK
KROW = PIECE // D
RPB_W = 2 * WIN_W - 1
SHIFTS = 2 * ROWS - 2
BIAS_STEPS = 4
SLIDE = 2 * GRID - 1
MASKED = -1e30


def dense_pieces(w_in, w_out, ffg, ffu, ffd, qkv, wo):
    def columns(w, c0, width=BANK):
        tiles = PIECE // width
        v = w.rearrange("(k p) n -> p k n", p=P)
        return [(v[:, k:k + tiles, c0:c0 + width], tiles, width) for k in range(0, KD, tiles)]

    def rows(w, r0, n_rows):
        v = w.rearrange("(k p) n -> p k n", p=P)
        return [(v[:, k:k + KROW, :], KROW, D) for k in range(r0 // P, (r0 + n_rows) // P, KROW)]

    out = {"w_in": [columns(w_in, c) for c in (0, BANK)], "w_out": [columns(w_out, c) for c in (0, BANK)],
           "qkv": [columns(qkv, c) for c in range(0, 3 * D, BANK)], "wo": [columns(wo, c) for c in (0, BANK)]}
    widths = [BANK] * (FF // BANK) + ([FF % BANK] if FF % BANK else [])
    out["gate"] = [columns(ffg, BANK * c, w) for c, w in enumerate(widths)]
    out["up"] = [columns(ffu, BANK * c, w) for c, w in enumerate(widths)]
    out["down"] = [rows(ffd, BANK * c, w) for c, w in enumerate(widths)]
    order = [x for k in ("w_in", "w_out") for x in out[k]]
    for c in range(len(widths)):
        order += [out["gate"][c], out["up"][c]]
        if c:
            order.append(out["down"][c - 1])
    order.append(out["down"][-1])
    order += out["qkv"]
    flat = [piece for group in order for piece in group]
    where = {}
    n = 0
    for group in order:
        where[id(group)] = list(range(n, n + len(group)))
        n += len(group)
    index = {k: [where[id(g)] for g in v] for k, v in out.items() if k != "wo"}
    flat += [out["wo"][c][half] for half in range(2) for c in range(2)]
    index["wo"] = [[n + c, n + 2 + c] for c in range(2)]
    return flat, index, widths


STEPS = FFE // BANK
def expert_pieces():
    order = []
    for c in range(STEPS):
        order += [("gate", c, 0), ("gate", c, 1), ("up", c, 0), ("up", c, 1)]
        if c:
            order += [("down", c - 1, 0), ("down", c - 1, 1)]
    order += [("down", STEPS - 1, 0), ("down", STEPS - 1, 1)]
    return order, {x: j for j, x in enumerate(order)}


PT = 4
EXPERT, AT = expert_pieces()
PER_EXPERT = len(EXPERT)
assert PER_EXPERT % RAW == 0 and PER_EXPERT % SPLIT == 0


def expert_source(ewg, ewu, ewd, e, j):
    kind, c, half = EXPERT[j]
    v = {"gate": ewg, "up": ewu, "down": ewd}[kind][0].rearrange("e (k p) n -> p (e k) n", p=P)
    if kind == "down":
        return v[:, bass.ds(e * (FFE // P) + (BANK // P * c + KROW * half), KROW), :], KROW, D
    return v[:, bass.ds(e * KD + KH * half, KH), BANK * c:BANK * (c + 1)], KH, BANK


def trunk(nc, x, norm_mix, norm_ffn, w_in, w_out, w_qkv, w_o, ffg, ffu, ffd, router_w, router_b,
          ewg, ewu, ewd, final_norm, gains_c, slide_c, dft_c, mask_c, ident_c, before_c, count_c, out):
    f32, f32r, bf16, i32 = mybir.dt.float32, mybir.dt.float32r, mybir.dt.bfloat16, mybir.dt.int32
    ALU, ACT, AX = mybir.AluOpType, mybir.ActivationFunctionType, mybir.AxisListType

    dense, at, widths = dense_pieces(w_in[0], w_out[0], ffg[0], ffu[0], ffd[0], w_qkv[0], w_o[0])
    N0 = len(dense)
    dense += [expert_source(ewg, ewu, ewd, 0, j) for j in range(SPLIT)]
    N1 = len(dense)

    def sb(name, shape, dt=f32):
        return nc.alloc_sbuf_tensor(name, shape, dt)

    raw = [sb(f"raw{i}", [P, PIECE]) for i in range(RAW)]
    w_hi = [sb(f"w_hi{i}", [P, PIECE], f32r) for i in range(SPLIT)]
    w_lo = [sb(f"w_lo{i}", [P, PIECE], f32r) for i in range(SPLIT)]
    h = sb("h", [P, NB, D])
    hn = sb("hn", [P, NB, D])
    gains = sb("gains", [P, 4, KD])
    mask = sb("mask", [P, GRID])
    act_hi = sb("act_hi", [P, KD, S], f32r)
    act_lo = sb("act_lo", [P, KD, S], f32r)
    ident = sb("ident", [P, P])
    sumsq = sb("sumsq", [P, 5, NB])
    rstd = sb("rstd", [P, 5, NB])
    half_power = sb("half_power", [P, NB])
    silu_g = [sb(f"silu_g{i}", [P, BANK]) for i in range(2)]
    hid = [sb(f"hid{i}", [P, BANK]) for i in range(2)]
    hidT_start = -(-nc.sbuf_base // 32) * 32
    hidT_hi = [sb(f"hidT_hi{i}", [P, BANK], f32r) for i in range(2)]
    hidT_lo = [sb(f"hidT_lo{i}", [P, BANK], f32r) for i in range(2)]

    def width_of(shape):
        return -(-4 * int(np.prod(shape[1:])) // 32) * 32

    def layout(entries, off):
        made = {}
        for name, shape, dt in entries:
            made[name] = nc.alloc_sbuf_tensor_at(name, shape, dt, offset=off)
            off += width_of(shape)
        return made

    bias_l = [("bias", [P, HEADS * SHIFTS, GRID], f32)]
    fourier_l = [("dft_hi", [P, NB, 3 * S], f32r), ("dft_lo", [P, NB, 3 * S], f32r),
                 ("u_hi", [P, NB, D], f32r), ("u_lo", [P, NB, D], f32r),
                 ("pt_lo", [P, PT, 2 * S], f32r), ("pt_hi", [P, PT, 2 * S], f32r)]
    attn_l = bias_l + [("qT", [P, KD, S], f32), ("kT", [P, KD, S], f32),
                       ("v", [P, NB, D], f32), ("probT", [P, 2, NB * S], f32), ("neg_max", [P, 2, NB], f32),
                       ("p_sum", [P, NB, HEADS], f32), ("p_inv", [P, NB, HEADS], f32)]
    moe_l = [("gain", [P, 2, D], f32), ("hn_hi", [P, NB, D], f32r), ("hn_lo", [P, NB, D], f32r), ("xg_hi", [P, KD, P], f32r),
             ("xg_lo", [P, KD, P], f32r), ("y_hi", [P, D], f32r), ("y_lo", [P, D], f32r), ("xg", [P, D], f32),
             ("sel", [P, NB, P], f32r), ("selT", [P, NB, P], f32r), ("rw", [P, KD, NE], f32), ("rw_hi", [P, KD, NE], f32r),
             ("rw_lo", [P, KD, NE], f32r), ("rb", [P, NE], f32), ("count", [P, S], f32), ("before", [P, P], f32),
             ("ones", [P, P], bf16), ("before_h", [P, P], bf16), ("logitT", [P, S], f32),
             ("logit", [P, NB, NE], f32), ("top", [P, 2, NB], f32), ("eq", [P, NB, NE], f32),
             ("cand", [P, NB, NE], f32), ("idx", [P, 2, NB], f32), ("first", [P, NB, NE], f32),
             ("second", [P, NB, NE], f32), ("rest", [P, NB, NE], f32), ("used", [P, NB, NE], bf16),
             ("gap", [P, NB], f32), ("ratio", [P, NB], f32), ("den", [P, NB], f32), ("g1", [P, NB], f32),
             ("g2", [P, NB], f32), ("weight", [P, NB, NE], f32), ("slot", [P, NB, 2 * NE], f32),
             ("most", [P, 1], f32), ("flag", [P, 1], i32)]
    arena_start = -(-nc.sbuf_base // 32) * 32
    sizes = [sum(width_of(shape) for _, shape, _ in l) for l in (fourier_l, attn_l, moe_l, bias_l + bias_l)]
    sb("arena", [P, max(sizes) // 4])
    fo, mo = (layout(l, arena_start) for l in (fourier_l, moe_l))
    behind_bias = arena_start + width_of(bias_l[0][1])
    att = layout(attn_l, arena_start)
    bias_raw = layout([("bias_raw", [P, HEADS * SHIFTS, GRID], f32)], behind_bias)["bias_raw"]
    fo |= layout([("dft_raw", [P, NB, 3 * S], f32)], arena_start + sum(width_of(shape) for _, shape, _ in fourier_l[:-1]))

    bank = {n: nc.alloc_psum_tensor(f"bank_{n}", [P, BANK], f32) for n in ("G0", "G1", "U0", "U1", "Y0", "Y1", "T0", "T1")}
    G, U, Y, T = ([bank[f"{n}0"], bank[f"{n}1"]] for n in "GUYT")

    def two(bk):
        return bk[:].rearrange("p (k s) -> p k s", k=2)

    def four(bk):
        return bk[:].rearrange("p (k s) -> p k s", k=4)

    def sem(name):
        return nc.alloc_semaphore(name)

    raw_in = [sem(f"raw_in{i}") for i in range(RAW)]
    hi_made, lo_made, piece_used, part_made = sem("hi_made"), sem("lo_made"), sem("piece_used"), sem("part_made")
    s_const, s_dft, s_mask, s_rout, s_gain, s_out = (sem(f"s_{n}") for n in ("const", "dft", "mask", "rout", "gain", "out"))
    s_bias = [sem(f"s_bias{step}") for step in range(BIAS_STEPS)]
    s_x = [sem(f"s_x{c}") for c in range(2)]
    h_half, sq_done, rstd_chain, rstd_done, hn_done = (sem(n) for n in (
        "h_half", "sq_done", "rstd_chain", "rstd_done", "hn_done"))
    tr_done, act_hi_done, act_lo_done = sem("tr_done"), sem("act_hi_done"), sem("act_lo_done")
    dft_hi_done, dft_lo_done, u_psum, u_hi_done, u_lo_done = (sem(n) for n in ("dft_hi_done", "dft_lo_done", "u_psum", "u_hi_done", "u_lo_done"))
    pt_psum, pt_hi_done, pt_lo_done, ft_psum, ft_hi_done, ft_lo_done, fo_psum = (sem(n) for n in (
        "pt_psum", "pt_hi_done", "pt_lo_done", "ft_psum", "ft_hi_done", "ft_lo_done", "fo_psum"))
    d_gate, d_silu, d_up, d_hid, d_hidT, d_hidT_hi, d_hidT_lo, d_down, d_added = (sem("d_" + n) for n in (
        "gate", "silu", "up", "hid", "hidT", "hidT_hi", "hidT_lo", "down", "added"))
    qkv_psum, qkv_act, qkv_dve, qkT_psum, qT_act, qT_dve = (sem(n) for n in (
        "qkv_psum", "qkv_act", "qkv_dve", "qkT_psum", "qT_act", "qT_dve"))
    bias_done, a_score, a_biased, a_max, a_exp, a_inv, a_pT, a_pTcopy, a_pv, a_out, a_oT, a_ohi, a_olo, ao_psum = (sem(n) for n in (
        "bias_done", "a_score", "a_biased", "a_max", "a_exp", "a_inv", "a_pT", "a_pTcopy", "a_pv", "a_out", "a_oT", "a_ohi", "a_olo", "ao_psum"))
    logitT_done, before_done, hnr_hi, hnr_lo, rw_hi_done, rw_lo_done, ones_done, logit_psum, gap_done, ratio_done, used_done, rank_psum, flag_done, dve_chain = (sem(n) for n in (
        "logitT_done", "before_done", "hnr_hi", "hnr_lo", "rw_hi_done", "rw_lo_done", "ones_done", "logit_psum", "gap_done", "ratio_done", "used_done", "rank_psum", "flag_done", "dve_chain"))
    e_xg_act, e_xg_dve, e_xT, e_silu, e_hid, e_hidT, e_hidT_hi, e_hidT_lo, e_selT, e_selT_copy, e_sel, e_gather, e_xhi, e_xlo, e_yhi, e_ylo, e_scatter, e_added = (
        sem("e_" + n) for n in ("xg_act", "xg_dve", "xT", "silu", "hid", "hidT", "hidT_hi", "hidT_lo", "selT", "selT_copy",
                                "sel", "gather", "xhi", "xlo", "yhi", "ylo", "scatter", "added"))
    e_y, moe_done, fin_gain, fin_act, fin_dve = (sem(n) for n in ("e_y", "moe_done", "fin_gain", "fin_act", "fin_dve"))

    W0 = at["wo"][0][0]
    DC = len(widths)
    EXPERTS = {0: (0, NE), 1: (NE, 2 * NE)}

    def piece(j, E, back=0):
        return j + 1 - back if E is None else E * PER_EXPERT + (N0 + j + 1 - back)

    def slot_of(j, E, n):
        return (j if E is None else N0 + j) % n

    def has_before(j, E, back):
        return E is not None or j >= back

    TY = [T[0], T[1], Y[0], Y[1]]
    STREAM = [TY, TY, TY, [G[0], G[1], U[0], Y[0]]]
    PARTS = PIECE // BANK
    FIRST_PART = 5
    OB = [U, Y]
    QK = layout([(f"qk{i}{b}", [P, BANK], f32) for i in range(2) for b in range(NB)], hidT_start)
    QK = [[QK[f"qk{i}{b}"] for b in range(NB)] for i in range(2)]
    OT = [U[0], Y[0], G[0], G[1]]
    WO = [[U[0], Y[0]], T]

    def HT(c):
        return G if c == DC - 1 else T

    def projected(eng, first_block, c, pieces, b):
        if b < NB - 1:
            eng.wait_ge(first_block, c + 1)
        else:
            eng.wait_ge(piece_used, pieces[-1] + 1)

    block = nc.Block()
    block.__enter__()

    @block.sync
    def _(sp):
        def load(j, E, src, tiles):
            s = slot_of(j, E, RAW)
            if has_before(j, E, RAW):
                sp.wait_ge(lo_made, piece(j, E, RAW))
            sp.dma_start(raw[s][:].rearrange("p (k n) -> p k n", k=tiles), src).then_inc(raw_in[s], 16)

        for c in range(2):
            cs = slice(BANK * c, BANK * (c + 1))
            sp.dma_start(h[:, :, cs], x[0, :, cs].rearrange("(b p) d -> p b d", p=P)).then_inc(s_x[c], 16)
        for j, (src, tiles, _) in enumerate(dense):
            load(j, None, src, tiles)
            if j == 3:
                sp.dma_start(fo["dft_raw"][:], dft_c.rearrange("(b p) n -> p b n", p=P)).then_inc(s_dft, 16)

        def expert_loads(E):
            for j in range(SPLIT, PER_EXPERT + SPLIT):
                e = E % NE if j < PER_EXPERT else (E + 1) % NE
                src, tiles, _ = expert_source(ewg, ewu, ewd, e, j % PER_EXPERT)
                load(j, E, src, tiles)

        with sp.Fori(*EXPERTS[0]) as E:
            expert_loads(E)
        sp.wait_ge(flag_done, 1)
        over = sp.value_load(mo["flag"][0:1, 0:1], min_val=0, max_val=1)
        with sp.If(over):
            with sp.Fori(*EXPERTS[1]) as E:
                expert_loads(E)
        for b in range(NB):
            sp.wait_ge((fin_act, fin_dve)[b], 1)
            sp.dma_start(out[0, P * b:P * (b + 1), :], hn[:, b, :]).then_inc(s_out, 16)
        sp.wait_ge(s_out, 16 * NB)

    @block.gpsimd
    def _(pool):
        def rstds(i):
            pool.wait_ge(sq_done, NB * (i + 1))
            nc.gpsimd.tensor_scalar(rstd[:, i], sumsq[:, i], 1.0 / D, EPS, ALU.mult, ALU.add).then_inc(rstd_chain, 1)
            pool.wait_ge(rstd_chain, i + 2)
            nc.gpsimd.tensor_tensor(rstd[:, i], rstd[:, i], half_power[:], ALU.pow).then_inc(rstd_done, 1)

        nc.gpsimd.memset(half_power[:], -0.5).then_inc(rstd_chain, 1)
        for i in range(3):
            rstds(i)
        pool.wait_ge(a_pv, HEADS)
        for n, g in enumerate((norm_ffn[1:2, :], final_norm.rearrange("(a n) -> a n", a=1))):
            pool.dma_start(mo["gain"][:, n], g.partition_broadcast(P).rearrange("p a n -> p (a n)")).then_inc(s_gain, 16)
        pool.dma_start(mo["rw"][:], router_w[0].rearrange("(k p) n -> p k n", p=P)).then_inc(s_rout, 16)
        pool.dma_start(mo["rb"][:], router_b[0:1, :].partition_broadcast(P).rearrange("p a n -> p (a n)")).then_inc(s_rout, 16)
        pool.dma_start(mo["before"][:], before_c).then_inc(s_rout, 16)
        pool.dma_start(mo["count"][:], count_c).then_inc(s_rout, 16)
        nc.gpsimd.memset(mo["ones"][:], 1.0).then_inc(ones_done, 1)
        nc.gpsimd.memset(mo["slot"][:], -1.0).then_inc(ones_done, 1)
        pool.wait_ge(s_gain, 32)
        for c in range(2):
            pool.wait_ge(h_half, 4 + c + 1)
            cs = slice(BANK * c, BANK * (c + 1))
            nc.gpsimd.tensor_tensor(hn[:, :, cs], h[:, :, cs], mo["gain"][:, 0:1, cs].to_broadcast([P, NB, BANK]),
                                    ALU.mult).then_inc(hn_done, 1)
        rstds(3)
        pool.wait_ge(moe_done, 1)
        nc.gpsimd.tensor_tensor(hn[:, 0], h[:, 0], mo["gain"][:, 1], ALU.mult).then_inc(fin_gain, 1)
        rstds(4)

    @block.scalar
    def _(act):
        made = [0]

        def split_hi(j, E):
            s, w = slot_of(j, E, RAW), slot_of(j, E, SPLIT)
            rounds = 16 * (j // RAW + 1) if E is None else 16 * ((N0 + j) // RAW + 1) + E * (16 * PER_EXPERT // RAW)
            act.wait_ge(raw_in[s], rounds)
            if has_before(j, E, SPLIT):
                act.wait_ge(piece_used, piece(j, E, SPLIT))
            nc.scalar.activation(w_hi[w][:], raw[s][:], ACT.Copy).then_inc(hi_made, 1)

        def split_part(j, part):
            s, w, cs = slot_of(j, None, RAW), slot_of(j, None, SPLIT), slice(BANK * part, BANK * (part + 1))
            if part == 0:
                act.wait_ge(raw_in[s], 16 * (j // RAW + 1))
                if has_before(j, None, SPLIT):
                    act.wait_ge(piece_used, piece(j, None, SPLIT))
            last = nc.scalar.activation(w_hi[w][:, cs], raw[s][:, cs], ACT.Copy)
            if part < PARTS - 1:
                last.then_inc(part_made, 1)
            else:
                last.then_inc(hi_made, 1)
                made[0] += 1

        def split_past(n):
            while made[0] < min(n + SPLIT, N1):
                split_hi(made[0], None)
                made[0] += 1

        whole = [(s_x[1], 16), (h_half, 2), (h_half, 4), (h_half, 6), (moe_done, 1)]

        def squares(i):
            act.wait_ge(*whole[i])
            if i == 0:
                act.wait_ge(s_x[0], 16)
            for b in range(NB):
                terms = mo["hn_hi"] if i >= 3 else hn
                nc.scalar.activation(terms[:, b], h[:, b], ACT.Square, accum_out=sumsq[:, i, b:b + 1]).then_inc(sq_done, 1)

        def stream_hi(i, half):
            for q in (2 * half, 2 * half + 1):
                act.wait_ge(tr_done, 4 * i + q + 1)
                for k in range(2):
                    last = nc.scalar.activation(act_hi[:, 2 * q + k], two(STREAM[i][q])[:, k], ACT.Copy,
                                                scale=gains[:, i, 2 * q + k:2 * q + k + 1])
                last.then_inc(act_hi_done, 1)

        act.dma_start(ident[:], ident_c).then_inc(s_const, 16)
        act.dma_start(gains[:], gains_c).then_inc(s_const, 16)
        act.dma_start(mask[:], mask_c).then_inc(s_mask, 16)
        act.wait_ge(rstd_chain, 1)
        nc.scalar.activation(silu_g[0][:, :NB], half_power[:], ACT.Copy)
        act.wait_ge(s_const, 32)
        stream_hi(0, 0)
        stream_hi(0, 1)
        for part in range(PARTS):
            split_part(0, part)
        split_past(0)
        squares(0)
        act.wait_ge(rstd_done, 1)
        for c in range(2):
            split_past(at["w_in"][c][-1])
            for b in range(NB):
                projected(act, u_psum, c, at["w_in"][c], b)
                nc.scalar.activation(fo["u_hi"][:, b, BANK * c:BANK * (c + 1)], (G, U)[c][b][:], ACT.Copy,
                                     scale=rstd[:, 0, b:b + 1]).then_inc(u_hi_done, 1)
            if c == 0:
                act.wait_ge(s_dft, 16)
                nc.scalar.activation(fo["dft_hi"][:], fo["dft_raw"][:], ACT.Copy).then_inc(dft_hi_done, 1)
        for g in range(KD // 2 + 1):
            for m in (2 * g, 2 * g + 1) if g < KD // 2 else ():
                act.wait_ge(pt_psum, m + 1)
                if m >= PT:
                    act.wait_ge(ft_psum, m // 2 * 2 - PT + 2)
                nc.scalar.activation(fo["pt_hi"][:, m % PT], T[m % 2][:], ACT.Copy).then_inc(pt_hi_done, 1)
            for m in (2 * g - 2, 2 * g - 1) if g else ():
                act.wait_ge(ft_psum, m + 1)
                nc.scalar.activation(act_hi[:, m], Y[m % 2][:, :S], ACT.Copy).then_inc(ft_hi_done, 1)
        split_past(at["w_out"][0][-1] + 1)
        stream_hi(1, 0)
        split_past(at["w_out"][1][-1])
        stream_hi(1, 1)
        split_past(at["w_out"][1][-1] + 1)
        squares(1)
        def load_bias(step):
            half, rows = step // 2, HEADS * SHIFTS // 2
            r0 = rows * (step % 2)
            src = slide_c[half, r0:r0 + rows, 0:GRID]
            src = bass.AP(src.tensor, src.offset, [[1, GRID], [SLIDE, rows], [1, GRID]])
            act.dma_start(bias_raw[GRID * half:GRID * (half + 1), r0:r0 + rows], src).then_inc(s_bias[step], 16)

        def dense_hidden_hi(c, blocks=range(NB)):
            for b in blocks:
                act.wait_ge(d_hidT, NB * c + b + 1)
                if c:
                    projected(act, d_down, c - 1, at["down"][c - 1], b)
                nc.scalar.activation(hidT_hi[b][:, :widths[c]], HT(c)[b][:, :widths[c]], ACT.Copy).then_inc(d_hidT_hi, 1)

        act.wait_ge(rstd_done, 2)
        for c in range(DC):
            w = widths[c]
            split_past(at["gate"][c][-1])
            for b in range(NB):
                projected(act, d_gate, c, at["gate"][c], b)
                if c:
                    act.wait_ge(d_hid, NB * (c - 1) + b + 1)
                nc.scalar.activation(silu_g[b][:, :w], G[b][:, :w], ACT.Silu, scale=rstd[:, 1, b:b + 1]).then_inc(d_silu, 1)
            if c:
                dense_hidden_hi(c - 1)
            split_past(at["up"][c][-1])
            if c < BIAS_STEPS:
                load_bias(c)
            if 0 < c < DC - 1:
                split_past(at["down"][c - 1][-1])
        n = at["down"][-1][-1]
        split_past(n - 2)
        dense_hidden_hi(DC - 1, [0])
        split_past(n - 1)
        dense_hidden_hi(DC - 1, [1])
        split_past(n)
        stream_hi(2, 0)
        stream_hi(2, 1)
        split_past(at["down"][-1][-1] + 1)
        squares(2)
        act.wait_ge(rstd_done, 3)
        act.wait_ge(bias_done, BIAS_STEPS)
        def output_hi(q):
            act.wait_ge(a_oT, q + 1)
            nc.scalar.activation(act_hi[:, 2 * q:2 * q + 2], two(OT[q]), ACT.Copy).then_inc(a_ohi, 1)

        for c in range(5):
            split_past(at["qkv"][c][-1])
            projected(act, qkv_psum, c, at["qkv"][c], 0)
            if 2 <= c < 4:
                act.wait_ge(qkT_psum, 2 * (c - 1))
            dst = QK[c % 2][0][:] if c < 4 else att["v"][:, 0, BANK * (c - 4):BANK * (c - 3)]
            nc.scalar.activation(dst, (G, U)[c % 2][0][:], ACT.Copy, scale=rstd[:, 2, 0:1]).then_inc(qkv_act, 1)
            if 1 <= c < 5:
                act.wait_ge(qkT_psum, 2 * c - 1)
                dst = att["qT"] if c < 3 else att["kT"]
                m = 4 * ((c - 1) % 2)
                nc.scalar.activation(dst[:, m:m + 2], two((T, Y)[(c - 1) % 2][0]), ACT.Copy).then_inc(qT_act, 1)
        split_past(W0 - 2)
        for i in range(HEADS + 2):
            if 2 <= i < HEADS + 2:
                g = i - 2
                act.wait_ge(a_pT, g + 1)
                if g >= 2:
                    act.wait_ge(a_pv, g - 1)
                nc.scalar.activation(att["probT"][:, g % 2], T[g % 2][:], ACT.Copy).then_inc(a_pTcopy, 1)
            if i < HEADS:
                act.wait_ge(a_max, i + 1)
                for b in range(NB):
                    last = nc.scalar.activation(hid[i % 2][:, S * b:S * (b + 1)], silu_g[i % 2][:, S * b:S * (b + 1)],
                                                ACT.Exp, bias=att["neg_max"][:, i % 2, b:b + 1],
                                                accum_out=att["p_sum"][:, NB - 1 - b, i:i + 1])
                    last.then_inc(a_exp, 1)
            if i == 3:
                projected(act, qkv_psum, 5, at["qkv"][5], 0)
                nc.scalar.activation(att["v"][:, 0, BANK:], U[1][:], ACT.Copy, scale=rstd[:, 2, 0:1]).then_inc(qkv_act, 1)
            if 0 <= i - FIRST_PART < PARTS:
                split_part(W0 + 1, i - FIRST_PART)
            if i in (HEADS - 3, HEADS - 2):
                output_hi(i - (HEADS - 3))
        split_past(W0)
        output_hi(2)
        output_hi(3)
        split_past(W0 + 1)
        act.wait_ge(s_rout, 64)
        nc.scalar.activation(mo["rw_hi"][:], mo["rw"][:], ACT.Copy).then_inc(rw_hi_done, 1)
        split_past(W0 + 2)
        stream_hi(3, 0)
        stream_hi(3, 1)
        squares(3)
        act.wait_ge(rstd_done, 4)
        act.wait_ge(hn_done, 2)
        for b in range(NB):
            nc.scalar.activation(mo["hn_hi"][:, b], hn[:, b], ACT.Copy, scale=rstd[:, 3, b:b + 1]).then_inc(hnr_hi, 1)
        split_past(W0 + 4)
        act.wait_ge(gap_done, 1)
        nc.scalar.activation(mo["ratio"][:], mo["gap"][:], ACT.Exp).then_inc(ratio_done, 1)

        def gather_copy(E1):
            act.wait_ge(e_gather, 2 * E1 - 1)
            nc.scalar.activation(mo["xg"][:, :BANK], G[1][:], ACT.Copy).then_inc(e_xg_act, 1)

        def gather_hi(E1):
            for q in range(2):
                act.wait_ge(e_xT, 2 * E1 - 1 + q)
                nc.scalar.activation(mo["xg_hi"][:, 4 * q:4 * q + 4], four((G, U)[q][1]), ACT.Copy).then_inc(e_xhi, 1)

        def silu(E, c):
            act.wait_ge(piece_used, piece(AT["gate", c, 1], E))
            if c != 1:
                act.wait_ge(e_hid, E * STEPS + max(c - 1, 0))
            nc.scalar.activation(silu_g[c % 2][:], G[c % 2][:], ACT.Silu).then_inc(e_silu, 1)

        def hidden_hi(E, c):
            act.wait_ge(e_hidT, E * STEPS + (c + 1))
            if c != 1:
                act.wait_ge(piece_used, piece(AT["down", c - 2, 1] if c else -1, E))
            nc.scalar.activation(hidT_hi[c % 2][:], T[c % 2][:], ACT.Copy).then_inc(e_hidT_hi, 1)

        def result_hi(E):
            for q in range(2):
                if q == 0:
                    act.wait_ge(e_y, E + 1)
                else:
                    act.wait_ge(piece_used, piece(PER_EXPERT - 1, E))
                nc.scalar.activation(mo["y_hi"][:, BANK * q:BANK * (q + 1)], Y[q][:], ACT.Copy).then_inc(e_yhi, 1)

        def expert(E, sweep):
            for j, (kind, c, half) in enumerate(EXPERT):
                if (kind, half) == ("gate", 1):
                    silu(E, c)
                    if c:
                        hidden_hi(E, c - 1)
                if (kind, c, half) == ("up", STEPS - 1, 1):
                    gather_copy(E + (sweep + 2))
                if (kind, c, half) == ("down", STEPS - 2, 0):
                    gather_hi(E + (sweep + 2))
                    hidden_hi(E, STEPS - 1)
                if (kind, c, half) == ("down", STEPS - 1, 1):
                    result_hi(E)
                split_hi(j + SPLIT, E)

        gather_copy(1)
        gather_hi(1)
        assert made[0] == N1
        with act.Fori(*EXPERTS[0]) as E:
            expert(E, 0)
        act.wait_ge(flag_done, 1)
        over = act.value_load(mo["flag"][0:1, 0:1], min_val=0, max_val=1)
        with act.If(over):
            gather_copy(NE + 2)
            gather_hi(NE + 2)
            with act.Fori(*EXPERTS[1]) as E:
                expert(E, 1)
        squares(4)
        act.wait_ge(rstd_done, 5)
        act.wait_ge(fin_gain, 1)
        nc.scalar.activation(hn[:, 0], hn[:, 0], ACT.Copy, scale=rstd[:, 4, 0:1]).then_inc(fin_act, 1)

    @block.vector
    def _(dve):
        made = [0]
        chain = [0]

        def link(ins):
            chain[0] += 1
            ins.then_inc(dve_chain, 1)
            dve.wait_ge(dve_chain, chain[0])

        def split_lo(j, E):
            s, w = slot_of(j, E, RAW), slot_of(j, E, SPLIT)
            dve.wait_ge(hi_made, piece(j, E))
            nc.vector.tensor_tensor(w_lo[w][:], raw[s][:], w_hi[w][:].bitcast(f32), ALU.subtract).then_inc(lo_made, 1)

        def split_part(j, part):
            s, w, cs = slot_of(j, None, RAW), slot_of(j, None, SPLIT), slice(BANK * part, BANK * (part + 1))
            if part < PARTS - 1:
                dve.wait_ge(part_made, (PARTS - 1 if j else 0) + part + 1)
            else:
                dve.wait_ge(hi_made, piece(j, None))
            last = nc.vector.tensor_tensor(w_lo[w][:, cs], raw[s][:, cs], w_hi[w][:, cs].bitcast(f32), ALU.subtract)
            if part == PARTS - 1:
                last.then_inc(lo_made, 1)
                made[0] += 1

        def split_past(n):
            while made[0] < min(n + SPLIT, N1):
                split_lo(made[0], None)
                made[0] += 1

        def rest(out_, whole, hi):
            return nc.vector.tensor_tensor(out_, whole, hi.bitcast(f32), ALU.subtract)

        def rest_scaled(out_, whole, scale, hi):
            return nc.vector.scalar_tensor_tensor(out=out_, in0=whole, scalar=scale, in1=hi.bitcast(f32),
                                                  op0=ALU.mult, op1=ALU.subtract)

        def stream_lo(i, half):
            for q in (2 * half, 2 * half + 1):
                dve.wait_ge(act_hi_done, 4 * i + q + 1)
                for k in range(2):
                    kk = 2 * q + k
                    last = rest_scaled(act_lo[:, kk], two(STREAM[i][q])[:, k], gains[:, i, kk:kk + 1], act_hi[:, kk])
                last.then_inc(act_lo_done, 1)

        def add_projection(pieces, psum, banks, c):
            for b in range(NB):
                projected(dve, psum, c, pieces[c], b)
                part = h[:, b, BANK * c:BANK * (c + 1)]
                last = nc.vector.tensor_tensor(part, banks[b][:], part, ALU.add)
            last.then_inc(h_half, 1)

        def mask_bias(step):
            half, rows = step // 2, HEADS * SHIFTS // 2
            p0, r0 = GRID * half, rows * (step % 2)
            dve.wait_ge(s_bias[step], 16)
            if step == 0:
                dve.wait_ge(s_mask, 16)
            full = [GRID, rows, GRID]
            a = bias_raw[p0:p0 + GRID, r0:r0 + rows]
            back = bass.AP(a.tensor, a.offset + GRID - 1, [a.ap[0], [GRID, rows], [-1, GRID]])
            nc.vector.tensor_tensor(att["bias"][p0:p0 + GRID, r0:r0 + rows], back,
                                    mask[p0:p0 + GRID].unsqueeze(1).to_broadcast(full), ALU.add).then_inc(bias_done, 1)

        dve.wait_ge(s_const, 32)
        stream_lo(0, 0)
        stream_lo(0, 1)
        for part in range(PARTS):
            split_part(0, part)
        split_past(0)
        dve.wait_ge(rstd_done, 1)
        for c in range(2):
            split_past(at["w_in"][c][-1])
            for b in range(NB):
                dve.wait_ge(u_hi_done, NB * c + b + 1)
                cs = slice(BANK * c, BANK * (c + 1))
                rest_scaled(fo["u_lo"][:, b, cs], (G, U)[c][b][:], rstd[:, 0, b:b + 1], fo["u_hi"][:, b, cs]).then_inc(u_lo_done, 1)
            if c == 0:
                dve.wait_ge(dft_hi_done, 1)
                rest(fo["dft_lo"][:], fo["dft_raw"][:], fo["dft_hi"][:]).then_inc(dft_lo_done, 1)
        for g in range(KD // 2 + 1):
            for m in (2 * g, 2 * g + 1) if g < KD // 2 else ():
                dve.wait_ge(pt_hi_done, m + 1)
                rest(fo["pt_lo"][:, m % PT], T[m % 2][:], fo["pt_hi"][:, m % PT]).then_inc(pt_lo_done, 1)
            for m in (2 * g - 2, 2 * g - 1) if g else ():
                dve.wait_ge(ft_hi_done, m + 1)
                rest(act_lo[:, m], Y[m % 2][:, :S], act_hi[:, m]).then_inc(ft_lo_done, 1)
        n = at["w_out"][0][-1]
        split_past(n)
        add_projection(at["w_out"], fo_psum, G, 0)
        split_past(n + 1)
        stream_lo(1, 0)
        split_past(n + 2)
        add_projection(at["w_out"], fo_psum, U, 1)
        stream_lo(1, 1)
        split_past(n + 3)

        def hidden_lo(c, blocks=range(NB)):
            for b in blocks:
                dve.wait_ge(d_hidT_hi, NB * c + b + 1)
                rest(hidT_lo[b][:, :widths[c]], HT(c)[b][:, :widths[c]], hidT_hi[b][:, :widths[c]]).then_inc(d_hidT_lo, 1)

        def add_down(c, blocks=range(NB)):
            for b in blocks:
                projected(dve, d_down, c, at["down"][c], b)
                for q in range(2):
                    part = h[:, b, BANK * q:BANK * (q + 1)]
                    last = nc.vector.tensor_tensor(part, (Y, T)[b][q][:], part, ALU.add)
                last.then_inc(d_added, 1)

        dve.wait_ge(rstd_done, 2)
        for c in range(DC):
            w = widths[c]
            split_past(at["gate"][c][-1])
            if c:
                hidden_lo(c - 1)
            split_past(at["up"][c][-1])
            for b in range(NB):
                dve.wait_ge(d_silu, NB * c + b + 1)
                projected(dve, d_up, c, at["up"][c], b)
                if c:
                    dve.wait_ge(d_hidT, NB * (c - 1) + b + 1)
                nc.vector.scalar_tensor_tensor(out=hid[b][:, :w], in0=U[b][:, :w], scalar=rstd[:, 1, b:b + 1],
                                               in1=silu_g[b][:, :w], op0=ALU.mult, op1=ALU.mult).then_inc(d_hid, 1)
            if 0 < c < DC - 1:
                split_past(at["down"][c - 1][-1])
                add_down(c - 1)
                if c <= BIAS_STEPS:
                    mask_bias(c - 1)
        n = at["down"][-1][-1]
        split_past(n - 2)
        add_down(DC - 2, [0])
        hidden_lo(DC - 1, [0])
        hidden_lo(DC - 1, [1])
        add_down(DC - 2, [1])
        dve.wait_ge(d_added, NB * (DC - 1))
        for q in range(2):
            projected(dve, d_down, DC - 1, at["down"][-1], q)
            for b in range(NB):
                part = h[:, b, BANK * q:BANK * (q + 1)]
                last = nc.vector.tensor_tensor(part, (Y, U)[b][q][:], part, ALU.add)
            last.then_inc(h_half, 1)
            split_past(n - 1 + q)
            stream_lo(2, q)
        split_past(n + 1)
        dve.wait_ge(rstd_done, 3)
        for c in range(5):
            split_past(at["qkv"][c][-1])
            projected(dve, qkv_psum, c, at["qkv"][c], 1)
            if 2 <= c < 4:
                dve.wait_ge(qkT_psum, 2 * (c - 1))
            dst = QK[c % 2][1][:] if c < 4 else att["v"][:, 1, BANK * (c - 4):BANK * (c - 3)]
            nc.vector.tensor_scalar(dst, (G, U)[c % 2][1][:], rstd[:, 2, 1:2], None, ALU.mult).then_inc(qkv_dve, 1)
            if 1 <= c < 5:
                dve.wait_ge(qkT_psum, 2 * c)
                dst = att["qT"] if c < 3 else att["kT"]
                m = 4 * ((c - 1) % 2)
                nc.vector.tensor_copy(dst[:, m + 2:m + 4], two((T, Y)[(c - 1) % 2][1])).then_inc(qT_dve, 1)
        def head_bias(i):
            a = att["bias"][:, SHIFTS * i:SHIFTS * (i + 1)]
            return bass.AP(a.tensor, a.offset, [a.ap[0], [(ROWS - 2) * GRID, NB], [1, S]])

        dve.wait_ge(bias_done, BIAS_STEPS)
        def output(hg, b):
            hs = slice(HEADS // 2 * hg, HEADS // 2 * (hg + 1))
            if b == 0:
                dve.wait_ge(a_exp, NB * HEADS // 2 * (hg + 1))
                nc.vector.reciprocal(att["p_inv"][:, :, hs], att["p_sum"][:, :, hs]).then_inc(a_inv, 1)
                dve.wait_ge(a_inv, hg + 1)
                dve.wait_ge(a_pv, HEADS // 2 * (hg + 1))
            last = nc.vector.tensor_tensor(hn[:, b, BANK * hg:BANK * (hg + 1)].rearrange("p (h d) -> p h d", d=HD),
                                               OB[b][hg][:].rearrange("p (h d) -> p h d", d=HD),
                                               att["p_inv"][:, b, hs].unsqueeze(2).to_broadcast([P, HEADS // 2, HD]), ALU.mult)
            last.then_inc(a_out, 1)

        def output_lo(q):
            dve.wait_ge(a_ohi, q + 1)
            rest(act_lo[:, 2 * q:2 * q + 2], two(OT[q]), act_hi[:, 2 * q:2 * q + 2]).then_inc(a_olo, 1)

        split_past(W0 - 2)
        for i in range(HEADS):
            dve.wait_ge(a_score, i + 1)
            if i >= 2:
                dve.wait_ge(a_exp, NB * (i - 1))
            nc.vector.scalar_tensor_tensor(out=silu_g[i % 2][:].rearrange("p (n k) -> p n k", n=NB), in0=two(G[i % 2]),
                                           scalar=float(HD) ** -0.5, in1=head_bias(i), op0=ALU.mult, op1=ALU.add).then_inc(a_biased, 1)
            dve.wait_ge(a_biased, i + 1)
            nc.vector.tensor_reduce(att["neg_max"][:, i % 2], silu_g[i % 2][:].rearrange("p (b k) -> p b k", b=NB),
                                    AX.X, ALU.max, negate=True).then_inc(a_max, 1)
            if i == 3:
                projected(dve, qkv_psum, 5, at["qkv"][5], 1)
                nc.vector.tensor_scalar(att["v"][:, 1, BANK:], Y[1][:], rstd[:, 2, 1:2], None, ALU.mult).then_inc(qkv_dve, 1)
            if 0 <= i - FIRST_PART - 1 < PARTS:
                split_part(W0 + 1, i - FIRST_PART - 1)
            if i - (HEADS // 2 + 2) in range(NB):
                output(0, i - (HEADS // 2 + 2))
            if i in (HEADS - 2, HEADS - 1):
                output_lo(i - (HEADS - 2))
        split_past(W0)
        for b in range(NB):
            output(1, b)
        output_lo(2)
        output_lo(3)
        split_past(W0 + 1)
        dve.wait_ge(rw_hi_done, 1)
        rest(mo["rw_lo"][:], mo["rw"][:], mo["rw_hi"][:]).then_inc(rw_lo_done, 1)
        add_projection(at["wo"], ao_psum, WO[0], 0)
        split_past(W0 + 2)
        stream_lo(3, 0)
        add_projection(at["wo"], ao_psum, WO[1], 1)
        stream_lo(3, 1)

        dve.wait_ge(s_rout, 64)
        nc.vector.tensor_copy(mo["before_h"][:], mo["before"][:]).then_inc(before_done, 1)
        dve.wait_ge(logit_psum, 1)
        nc.vector.tensor_copy(mo["logitT"][:NE], G[0][:NE, :S]).then_inc(logitT_done, 1)
        def token_rest(b):
            dve.wait_ge(hnr_hi, b + 1)
            rest_scaled(mo["hn_lo"][:, b], hn[:, b], rstd[:, 3, b:b + 1], mo["hn_hi"][:, b]).then_inc(hnr_lo, 1)

        dve.wait_ge(rstd_done, 4)
        dve.wait_ge(logit_psum, 2)
        full = [P, NB, NE]

        def each_token(t):
            return t.unsqueeze(2).to_broadcast(full)

        iota = mo["count"][:, 0:NE].unsqueeze(1).to_broadcast(full)
        for b in range(NB):
            link(nc.vector.scalar_tensor_tensor(out=mo["logit"][:, b], in0=G[1][:, NE * b:NE * (b + 1)], scalar=rstd[:, 3, b:b + 1],
                                                in1=mo["rb"][:], op0=ALU.mult, op1=ALU.add))
        for n, (src, one) in enumerate((("logit", "first"), ("rest", "second"))):
            link(nc.vector.tensor_reduce(mo["top"][:, n], mo[src][:], AX.X, ALU.max))
            link(nc.vector.tensor_tensor(mo["eq"][:], mo[src][:], each_token(mo["top"][:, n]), ALU.is_equal))
            link(nc.vector.scalar_tensor_tensor(out=mo["cand"][:], in0=iota, scalar=-float(NE), in1=mo["eq"][:],
                                                op0=ALU.add, op1=ALU.mult))
            link(nc.vector.tensor_reduce(mo["idx"][:, n], mo["cand"][:], AX.X, ALU.min))
            link(nc.vector.tensor_scalar(mo["idx"][:, n], mo["idx"][:, n], float(NE), None, ALU.add))
            link(nc.vector.tensor_tensor(mo[one][:], iota, each_token(mo["idx"][:, n]), ALU.is_equal))
            if n == 0:
                link(nc.vector.scalar_tensor_tensor(out=mo["rest"][:], in0=mo["first"][:], scalar=-3e38,
                                                    in1=mo["logit"][:], op0=ALU.mult, op1=ALU.add))
        nc.vector.tensor_tensor(mo["used"][:], mo["first"][:], mo["second"][:], ALU.add).then_inc(used_done, 1)
        nc.vector.tensor_tensor(mo["gap"][:], mo["top"][:, 1], mo["top"][:, 0], ALU.subtract).then_inc(gap_done, 1)
        dve.wait_ge(used_done, 1)
        dve.wait_ge(rank_psum, 1)
        dve.wait_ge(ones_done, 2)
        slots = mo["slot"][:, :, 0:NE]
        link(nc.vector.scalar_tensor_tensor(out=slots, in0=T[1][:, 0:NB * NE].rearrange("p (b e) -> p b e", b=NB),
                                            scalar=1.0, in1=mo["used"][:], op0=ALU.add, op1=ALU.mult))
        link(nc.vector.tensor_scalar(slots, slots, -1.0, None, ALU.add))

        def gather_copy(E1):
            dve.wait_ge(e_gather, 2 * E1)
            nc.vector.tensor_copy(mo["xg"][:, BANK:], U[1][:]).then_inc(e_xg_dve, 1)

        def gather_lo(E1):
            for q in range(2):
                dve.wait_ge(e_xhi, 2 * E1 - 1 + q)
                rest(mo["xg_lo"][:, 4 * q:4 * q + 4], four((G, U)[q][1]), mo["xg_hi"][:, 4 * q:4 * q + 4]).then_inc(e_xlo, 1)

        def select(sweep, e):
            for b in range(NB):
                last = nc.vector.tensor_scalar(mo["sel"][:, b], mo["count"][:, P * sweep:P * (sweep + 1)],
                                               mo["slot"][:, b, bass.ds(e, 1)], None, ALU.is_equal)
            last.then_inc(e_sel, 1)

        def hidden(E, c):
            dve.wait_ge(e_silu, E * STEPS + (c + 1))
            dve.wait_ge(piece_used, piece(AT["up", c, 1], E))
            if c != 1:
                dve.wait_ge(e_hidT, E * STEPS + max(c - 1, 0))
            nc.vector.tensor_tensor(hid[c % 2][:], U[c % 2][:], silu_g[c % 2][:], ALU.mult).then_inc(e_hid, 1)

        def hidden_rest(E, c):
            dve.wait_ge(e_hidT_hi, E * STEPS + (c + 1))
            rest(hidT_lo[c % 2][:], T[c % 2][:], hidT_hi[c % 2][:]).then_inc(e_hidT_lo, 1)

        def next_selection(E, e, sweep):
            dve.wait_ge(e_selT, E + 1)
            dve.wait_ge(e_scatter, 2 * E)
            nc.vector.tensor_copy(mo["selT"][:], T[1][:, :NB * P].rearrange("p (b t) -> p b t", b=NB)).then_inc(e_selT_copy, 1)
            select(sweep, e + 1)

        def result_rest(E):
            for q in range(2):
                dve.wait_ge(e_yhi, 2 * E + 1 + q)
                cs = slice(BANK * q, BANK * (q + 1))
                rest(mo["y_lo"][:, cs], Y[q][:], mo["y_hi"][:, cs]).then_inc(e_ylo, 1)

        def add_result(E, e):
            for q in range(2):
                dve.wait_ge(e_scatter, 2 * E + 1 + q)
                for b in range(NB):
                    part = h[:, b, BANK * q:BANK * (q + 1)]
                    src = T[q] if b == 0 else (G, U)[q][1]
                    last = nc.vector.scalar_tensor_tensor(out=part, in0=src[:], scalar=mo["weight"][:, b, bass.ds(e, 1)],
                                                          in1=part, op0=ALU.mult, op1=ALU.add)
            last.then_inc(e_added, 1)

        def expert(E, sweep):
            e = E - NE if sweep else E
            for j, (kind, c, half) in enumerate(EXPERT):
                if (kind, c, half) == ("gate", 0, 1):
                    next_selection(E, e, sweep)
                elif (kind, half) == ("gate", 1):
                    hidden_rest(E, c - 1)
                if (kind, half) == ("up", 1):
                    hidden(E, c)
                    if c == STEPS - 1:
                        gather_copy(E + (sweep + 2))
                if (kind, c, half) == ("down", STEPS - 2, 0):
                    gather_lo(E + (sweep + 2))
                    hidden_rest(E, STEPS - 1)
                if (kind, c, half) == ("down", STEPS - 1, 0):
                    continue
                if (kind, c, half) == ("down", STEPS - 1, 1):
                    result_rest(E)
                    split_lo(j - 1 + SPLIT, E)
                    add_result(E, e)
                split_lo(j + SPLIT, E)

        select(0, 0)
        token_rest(0)
        token_rest(1)
        link(nc.vector.tensor_reduce(mo["most"][:], T[1][:, NB * NE:(NB + 1) * NE], AX.X, ALU.max))
        nc.vector.tensor_scalar(mo["flag"][:], mo["most"][:], float(P), None, ALU.is_gt).then_inc(flag_done, 1)
        split_past(W0 + 3)
        gather_copy(1)
        gather_lo(1)
        split_past(W0 + 4)
        dve.wait_ge(ratio_done, 1)
        link(nc.vector.tensor_scalar(mo["den"][:], mo["ratio"][:], 1.0, None, ALU.add))
        link(nc.vector.reciprocal(mo["g1"][:], mo["den"][:]))
        link(nc.vector.tensor_tensor(mo["g2"][:], mo["ratio"][:], mo["g1"][:], ALU.mult))
        link(nc.vector.tensor_tensor(mo["first"][:], mo["first"][:], each_token(mo["g1"][:]), ALU.mult))
        link(nc.vector.tensor_tensor(mo["second"][:], mo["second"][:], each_token(mo["g2"][:]), ALU.mult))
        link(nc.vector.tensor_tensor(mo["weight"][:], mo["first"][:], mo["second"][:], ALU.add))
        assert made[0] == N1
        with dve.Fori(*EXPERTS[0]) as E:
            expert(E, 0)
        dve.wait_ge(flag_done, 1)
        over = dve.value_load(mo["flag"][0:1, 0:1], min_val=0, max_val=1)
        with dve.If(over):
            dve.wait_ge(e_gather, 2 * (NE + 1))
            select(1, 0)
            gather_copy(NE + 2)
            gather_lo(NE + 2)
            with dve.Fori(*EXPERTS[1]) as E:
                expert(E, 1)
            dve.wait_ge(e_added, 2 * NE)
        dve.wait_ge(e_added, NE)
        dve.sem_inc(moe_done, 1)
        dve.wait_ge(s_gain, 32)
        link(nc.vector.tensor_tensor(hn[:, 1], h[:, 1], mo["gain"][:, 1], ALU.mult))
        dve.wait_ge(rstd_done, 5)
        nc.vector.tensor_scalar(hn[:, 1], hn[:, 1], rstd[:, 4, 1:2], None, ALU.mult).then_inc(fin_dve, 1)

    @block.tensor
    def _(pe):
        def ready(j, E):
            pe.wait_ge(lo_made, piece(j, E))

        def parts(j, E, tiles):
            w = slot_of(j, E, SPLIT)
            return [t[:].rearrange("p (k n) -> p k n", k=tiles) for t in (w_hi[w], w_lo[w])]

        def three(out_, xh, xl, wh, wl, start, stop):
            nc.tensor.matmul(out_, xh, wh, start=start, stop=False)
            nc.tensor.matmul(out_, xh, wl, start=False, stop=False)
            return nc.tensor.matmul(out_, xl, wh, start=False, stop=stop)

        def project(pieces, banks, width, done, before=lambda n, b: None):
            for n, j in enumerate(pieces):
                tiles = PIECE // width
                ready(j, None)
                wh, wl = parts(j, None, tiles)
                for b in range(NB):
                    before(n, b)
                    for k in range(tiles):
                        kk = tiles * n + k
                        last = three(banks[b][:, :width], act_hi[:, kk, P * b:P * (b + 1)], act_lo[:, kk, P * b:P * (b + 1)],
                                     wh[:, k], wl[:, k], kk == 0, kk == KD - 1)
                    if n == len(pieces) - 1 and b < NB - 1:
                        last.then_inc(done, 1)
                last.then_inc(piece_used, 1)

        def transpose_stream(i, half):
            if i == 0:
                pe.wait_ge(s_x[half], 16)
            else:
                pe.wait_ge(h_half, 2 * (i - 1) + half + 1)
            for q in (2 * half, 2 * half + 1):
                for k in range(2):
                    for b in range(NB):
                        o = S * k + P * b
                        kk = 2 * q + k
                        last = nc.tensor.transpose(STREAM[i][q][:, o:o + P], h[:, b, P * kk:P * (kk + 1)], ident[:])
                last.then_inc(tr_done, 1)

        def stream_first(i):
            def before(n, b):
                if (n, b) == (1, 0):
                    transpose_stream(i, 0)
            return before

        def stream_second(i):
            def before(n, b):
                if (n, b) == (0, 0):
                    pe.wait_ge(act_lo_done, 4 * i + 2)
                if (n, b) == (0, 1) and i > 0:
                    transpose_stream(i, 1)
                if (n, b) == (1, 0):
                    pe.wait_ge(act_lo_done, 4 * i + 4)
            return before

        pe.wait_ge(s_const, 32)
        transpose_stream(0, 0)
        transpose_stream(0, 1)
        project(at["w_in"][0], G, BANK, u_psum, stream_second(0))
        project(at["w_in"][1], U, BANK, u_psum)
        pe.wait_ge(dft_lo_done, 1)
        def token_dft(m):
            if m == 0:
                pe.wait_ge(u_lo_done, NB)
            if m == KD // 2:
                pe.wait_ge(u_lo_done, 2 * NB)
            if m >= 2:
                pe.wait_ge(pt_lo_done, m - 1)
            for b in range(NB):
                last = three(T[m % 2][:], fo["u_hi"][:, b, P * m:P * (m + 1)], fo["u_lo"][:, b, P * m:P * (m + 1)],
                             fo["dft_hi"][:, b, 0:2 * S], fo["dft_lo"][:, b, 0:2 * S], b == 0, b == NB - 1)
            last.then_inc(pt_psum, 1)

        def channel_dft(m):
            g0 = m // 2 * 2
            pe.wait_ge(pt_lo_done, g0 + 2)
            if m >= 2:
                pe.wait_ge(ft_lo_done, m - 1)
            terms = [(k, part) for k in range(2) for part in range(2)]
            for n, (k, part) in enumerate(terms):
                o = (0, 2 * S)[part] + P * (m % 2)
                last = three(Y[m % 2][:, :S], fo["dft_hi"][:, k, o:o + P], fo["dft_lo"][:, k, o:o + P],
                             fo["pt_hi"][:, (g0 + k) % PT, S * part:S * (part + 1)],
                             fo["pt_lo"][:, (g0 + k) % PT, S * part:S * (part + 1)], n == 0, n == len(terms) - 1)
            last.then_inc(ft_psum, 1)

        for g in range(KD // 2 + 1):
            for m in (2 * g, 2 * g + 1) if g < KD // 2 else ():
                token_dft(m)
            for m in (2 * g - 2, 2 * g - 1) if g else ():
                channel_dft(m)
        pe.wait_ge(ft_lo_done, KD)
        project(at["w_out"][0], G, BANK, fo_psum)
        project(at["w_out"][1], U, BANK, fo_psum, stream_first(1))


        def hidden_transposes(c):
            for b in range(NB):
                pe.wait_ge(d_hid, NB * c + b + 1)
                if c and c < DC - 1:
                    pe.wait_ge(d_added, NB * c)
                for k in range(widths[c] // P):
                    last = nc.tensor.transpose(HT(c)[b][:, P * k:P * (k + 1)], hid[b][:, P * k:P * (k + 1)], ident[:])
                last.then_inc(d_hidT, 1)

        def down(c, between=lambda: None):
            pieces = at["down"][c]
            pe.wait_ge(d_hidT_lo, NB * (c + 1))
            for b in range(NB):
                if b:
                    between()
                if c:
                    pe.wait_ge(d_added, NB * (c - 1) + b + 1)
                for n, j in enumerate(pieces):
                    if b == 0:
                        ready(j, None)
                    wh, wl = parts(j, None, KROW)
                    for k in range(KROW):
                        kk = KROW * n + k
                        for q in range(2):
                            cs = slice(BANK * q, BANK * (q + 1))
                            last = three((Y, T)[b][q][:], hidT_hi[b][:, P * kk:P * (kk + 1)], hidT_lo[b][:, P * kk:P * (kk + 1)],
                                         wh[:, k, cs], wl[:, k, cs], kk == 0, kk == KROW * len(pieces) - 1)
                    if b == NB - 1:
                        last.then_inc(piece_used, 1)
                if b < NB - 1:
                    last.then_inc(d_down, 1)

        def last_down():
            (j,) = at["down"][DC - 1]
            ready(j, None)
            pe.wait_ge(d_added, NB * (DC - 2) + 1)
            wh, wl = parts(j, None, KROW)
            for q in range(2):
                for b in range(NB):
                    if (q, b) == (1, 1):
                        transpose_stream(2, 0)
                    if q == 0:
                        pe.wait_ge(d_hidT_lo, NB * (DC - 1) + b + 1)
                    for k in range(KROW):
                        last = three((Y, U)[b][q][:], hidT_hi[b][:, P * k:P * (k + 1)], hidT_lo[b][:, P * k:P * (k + 1)],
                                     wh[:, k, BANK * q:BANK * (q + 1)], wl[:, k, BANK * q:BANK * (q + 1)], k == 0, k == KROW - 1)
                last.then_inc((d_down, piece_used)[q], 1)

        for c in range(DC):
            if c == 0:
                project(at["gate"][0], G, widths[0], d_gate, stream_second(1))
            else:
                pe.wait_ge(d_silu, NB * c)
                project(at["gate"][c], G, widths[c], d_gate)
                hidden_transposes(c - 1)
                pe.wait_ge(d_hid, NB * c)
            project(at["up"][c], U, widths[c], d_up)
            if 0 < c < DC - 1:
                down(c - 1)
        down(DC - 2, lambda: hidden_transposes(DC - 1))
        last_down()


        def transpose_qk(c):
            pe.wait_ge(qkv_act, c + 1)
            pe.wait_ge(qkv_dve, c + 1)
            if c >= 2:
                pe.wait_ge(qT_act, c - 1)
                pe.wait_ge(qT_dve, c - 1)
            for t in range(2):
                for k in range(2):
                    for b in range(NB):
                        o = S * k + P * b
                        m = 2 * t + k
                        last = nc.tensor.transpose((T, Y)[c % 2][t][:, o:o + P], QK[c % 2][b][:, P * m:P * (m + 1)], ident[:])
                last.then_inc(qkT_psum, 1)

        for c in range(5):
            if c >= 2:
                pe.wait_ge(qkv_act, c - 1)
                pe.wait_ge(qkv_dve, c - 1)
            project(at["qkv"][c], (G, U)[c % 2], BANK, qkv_psum, stream_second(2) if c == 0 else lambda n, b: None)
            if c:
                transpose_qk(c - 1)

        def quarter(j, half, b, bk):
            ready(j, None)
            wh, wl = parts(j, None, KH)
            for k in range(KH):
                kk = KH * half + k
                last = three(bk[:], act_hi[:, kk, P * b:P * (b + 1)], act_lo[:, kk, P * b:P * (b + 1)],
                             wh[:, k], wl[:, k], kk == 0, kk == KD - 1)
            return last

        def v_product(half, b):
            last = quarter(at["qkv"][5][half], half, b, OB[b][1])
            if b == NB - 1:
                last.then_inc(piece_used, 1)
            elif half:
                last.then_inc(qkv_psum, 1)

        def outputs_transposed(half):
            pe.wait_ge(a_out, NB * (half + 1))
            for q in (2 * half, 2 * half + 1):
                for k in range(2):
                    for b in range(NB):
                        o, kk = S * k + P * b, 2 * q + k
                        last = nc.tensor.transpose(OT[q][:, o:o + P], hn[:, b, P * kk:P * (kk + 1)], ident[:])
                last.then_inc(a_oT, 1)

        def wo_product(c, half, b):
            pe.wait_ge(a_olo, 2 * half + 2)
            last = quarter(at["wo"][c][half], half, b, WO[c][b])
            if b == NB - 1:
                last.then_inc(piece_used, 1)
            elif half:
                last.then_inc(ao_psum, 1)

        pe.wait_ge(qkv_act, 4)
        pe.wait_ge(qT_dve, 2)
        v_product(0, 0)
        pe.wait_ge(qkv_act, 5)
        pe.wait_ge(qkv_dve, 5)
        pe.wait_ge(qT_act, 4)
        pe.wait_ge(qT_dve, 4)
        for i in range(HEADS + 3):
            if i < HEADS:
                m, p0 = i // 2, HD * (i % 2)
                if i >= 2:
                    pe.wait_ge(a_biased, i - 1)
                for b in range(NB):
                    n = NB - 1 - b
                    last = nc.tensor.matmul(G[i % 2][:, S * n:S * (n + 1)], att["qT"][p0:p0 + HD, m, P * b:P * (b + 1)],
                                            att["kT"][p0:p0 + HD, m, :], start=True, stop=True)
                last.then_inc(a_score, 1)
            if 2 <= i < HEADS + 2:
                g = i - 2
                pe.wait_ge(a_exp, NB * (g + 1))
                if g >= 2:
                    pe.wait_ge(a_pTcopy, g - 1)
                for k in range(NB):
                    for b in range(NB):
                        o, n = S * k + P * b, NB - 1 - b
                        last = nc.tensor.transpose(T[g % 2][:, o:o + P], hid[g % 2][:, S * n + P * k:S * n + P * (k + 1)], ident[:])
                last.then_inc(a_pT, 1)
            if i >= 3:
                g = i - 3
                pe.wait_ge(a_pTcopy, g + 1)
                if g == HEADS // 2:
                    pe.wait_ge(qkv_act, 6)
                    pe.wait_ge(qkv_dve, 6)
                o = HD * (g % (HEADS // 2))
                for b in range(NB):
                    for k in range(NB):
                        last = nc.tensor.matmul(OB[b][g // (HEADS // 2)][:, o:o + HD], att["probT"][:, g % 2, S * k + P * b:S * k + P * (b + 1)],
                                                att["v"][:, k, HD * g:HD * (g + 1)], start=(k == 0), stop=(k == NB - 1))
                last.then_inc(a_pv, 1)
            if i < 3:
                v_product((i + 1) // 2, (i + 1) % 2)
            if i == HEADS - 4:
                outputs_transposed(0)
            if i in (HEADS, HEADS + 1):
                wo_product(0, 0, i - HEADS)
        wo_product(1, 0, 0)
        outputs_transposed(1)
        wo_product(1, 0, 1)
        wo_product(0, 1, 0)
        wo_product(0, 1, 1)
        wo_product(1, 1, 0)
        transpose_stream(3, 0)
        wo_product(1, 1, 1)

        transpose_stream(3, 1)
        pe.wait_ge(rw_lo_done, 1)
        for k in range(KD):
            pe.wait_ge(act_lo_done, 4 * 3 + k // 2 + 1)
            last = three(G[0][:NE, :S], mo["rw_hi"][:, k], mo["rw_lo"][:, k], act_hi[:, k], act_lo[:, k], k == 0, k == KD - 1)
        last.then_inc(logit_psum, 1)
        pe.wait_ge(logitT_done, 1)
        for b in range(NB):
            last = nc.tensor.transpose(G[1][:, NE * b:NE * (b + 1)], mo["logitT"][:NE, P * b:P * (b + 1)], ident[:NE, :NE])
        last.then_inc(logit_psum, 1)
        pe.wait_ge(used_done, 1)
        pe.wait_ge(before_done, 1)
        pe.wait_ge(ones_done, 2)
        used = mo["used"][:].rearrange("p b e -> p (b e)")
        nc.tensor.matmul(T[1][:, 0:NE], mo["before_h"][:], used[:, 0:NE], start=True, stop=True)
        nc.tensor.matmul(T[1][:, NE:2 * NE], mo["before_h"][:], used[:, NE:2 * NE], start=True, stop=False)
        nc.tensor.matmul(T[1][:, NE:2 * NE], mo["ones"][:], used[:, 0:NE], start=False, stop=True)
        nc.tensor.matmul(T[1][:, 2 * NE:3 * NE], mo["ones"][:], used[:, 0:NE], start=True, stop=False)
        nc.tensor.matmul(T[1][:, 2 * NE:3 * NE], mo["ones"][:], used[:, NE:2 * NE], start=False, stop=True).then_inc(rank_psum, 1)

        def gather(E1=None):
            terms = [(part, b) for part in ("hn_hi", "hn_lo") for b in range(NB)]
            for n, (part, b) in enumerate(terms):
                if E1 == 1 and part == "hn_lo":
                    pe.wait_ge(hnr_lo, b + 1)
                for q in range(2):
                    last = nc.tensor.matmul((G, U)[q][1][:], mo["sel"][:, b], mo[part][:, b, BANK * q:BANK * (q + 1)],
                                            start=(n == 0), stop=(n == len(terms) - 1))
                    if n == len(terms) - 1:
                        last.then_inc(e_gather, 1)

        def transpose_tokens(E1):
            for q in range(2):
                pe.wait_ge((e_xg_act, e_xg_dve)[q], E1)
                for k in range(4):
                    kk = 4 * q + k
                    last = nc.tensor.transpose((G, U)[q][1][:, P * k:P * (k + 1)], mo["xg"][:, P * kk:P * (kk + 1)], ident[:])
                last.then_inc(e_xT, 1)

        def expert(E, sweep):
            def columns(kind, c, bk):
                for half in range(2):
                    j = AT[kind, c, half]
                    ready(j, E)
                    if (kind, c) == ("gate", 0):
                        pe.wait_ge(e_xlo, 2 * (E + sweep) + half + 1)
                    wh, wl = parts(j, E, KH)
                    for k in range(KH):
                        kk = KH * half + k
                        last = three(bk[:], mo["xg_hi"][:, kk], mo["xg_lo"][:, kk], wh[:, k], wl[:, k], kk == 0, kk == KD - 1)
                    last.then_inc(piece_used, 1)

            def hidden_transposes(c):
                pe.wait_ge(e_hid, E * STEPS + (c + 1))
                if c >= 2:
                    pe.wait_ge(e_hidT_lo, E * STEPS + (c - 1))
                if c == 1:
                    pe.wait_ge(e_selT_copy, E + 1)
                for k in range(BANK // P):
                    last = nc.tensor.transpose(T[c % 2][:, P * k:P * (k + 1)], hid[c % 2][:, P * k:P * (k + 1)], ident[:])
                last.then_inc(e_hidT, 1)

            def down(c, half):
                j = AT["down", c, half]
                ready(j, E)
                if half == 0:
                    pe.wait_ge(e_hidT_lo, E * STEPS + (c + 1))
                    if c == 0:
                        pe.wait_ge(e_ylo, 2 * E)
                wh, wl = parts(j, E, KROW)
                order = [(k, q) for k in range(KROW) for q in range(2)]
                if (c, half) == (STEPS - 1, 1):
                    order.sort(key=lambda kq: kq[1])
                for k, q in order:
                    kk = KROW * half + k
                    cs = slice(BANK * q, BANK * (q + 1))
                    last = three(Y[q][:], hidT_hi[c % 2][:, P * kk:P * (kk + 1)], hidT_lo[c % 2][:, P * kk:P * (kk + 1)],
                                 wh[:, k, cs], wl[:, k, cs], c == 0 and kk == 0, c == STEPS - 1 and kk == BANK // P - 1)
                    if (c, half, k, q) == (STEPS - 1, 1, KROW - 1, 0):
                        last.then_inc(e_y, 1)
                last.then_inc(piece_used, 1)

            for c in range(STEPS):
                if c == 0:
                    pe.wait_ge(e_silu, E * STEPS)
                elif c == 1:
                    pe.wait_ge(e_added, E)
                else:
                    pe.wait_ge(e_silu, E * STEPS + (c - 1))
                columns("gate", c, G[c % 2])
                if c == 0:
                    pe.wait_ge(e_added, E)
                    pe.wait_ge(e_sel, E + (sweep + 1))
                    for b in range(NB):
                        last = nc.tensor.transpose(T[1][:, P * b:P * (b + 1)], mo["sel"][:, b].bitcast(f32), ident[:])
                    last.then_inc(e_selT, 1)
                else:
                    hidden_transposes(c - 1)
                if c != 1:
                    pe.wait_ge(e_hid, E * STEPS + max(c - 1, 0))
                columns("up", c, U[c % 2])
                if 1 <= c < STEPS - 1:
                    down(c - 1, 0)
                    down(c - 1, 1)
            pe.wait_ge(e_sel, E + (sweep + 2))
            pe.wait_ge(e_hid, E * STEPS + (STEPS - 1))
            gather()
            down(STEPS - 2, 0)
            transpose_tokens(E + (sweep + 2))
            hidden_transposes(STEPS - 1)
            down(STEPS - 2, 1)
            down(STEPS - 1, 0)
            down(STEPS - 1, 1)
            pe.wait_ge(e_selT_copy, E + 1)
            pe.wait_ge(e_xlo, 2 * (E + (sweep + 2)))
            for q in range(2):
                pe.wait_ge(e_ylo, 2 * E + 1 + q)
                for b in range(NB):
                    cs = slice(BANK * q, BANK * (q + 1))
                    bk = T[q] if b == 0 else (G, U)[q][1]
                    nc.tensor.matmul(bk[:], mo["selT"][:, b], mo["y_hi"][:, cs], start=True, stop=False)
                    last = nc.tensor.matmul(bk[:], mo["selT"][:, b], mo["y_lo"][:, cs], start=False, stop=True)
                last.then_inc(e_scatter, 1)

        pe.wait_ge(hnr_hi, NB)
        pe.wait_ge(e_sel, 1)
        gather(1)
        transpose_tokens(1)
        with pe.Fori(*EXPERTS[0]) as E:
            expert(E, 0)
        pe.wait_ge(flag_done, 1)
        over = pe.value_load(mo["flag"][0:1, 0:1], min_val=0, max_val=1)
        with pe.If(over):
            pe.wait_ge(e_added, NE)
            pe.wait_ge(e_sel, NE + 2)
            gather()
            transpose_tokens(NE + 2)
            with pe.Fori(*EXPERTS[1]) as E:
                expert(E, 1)

    block.__exit__(None, None, None)


_INS = ["x", "norm_mix", "norm_ffn", "fourier_w_in", "fourier_w_out", "nat_w_qkv", "nat_w_o",
        "ffn_w_gate", "ffn_w_up", "ffn_w_down", "router_w", "router_b", "expert_w_gate", "expert_w_up",
        "expert_w_down", "final_norm"]
_OUTS = [((1, S, D), "float32")]


def shape_constants():
    turn = 2 * np.pi * (np.outer(np.arange(S), np.arange(S)) % S) / S
    cos, sin = np.cos(turn) / np.sqrt(S), np.sin(turn) / np.sqrt(S)
    dft = np.concatenate([cos, sin, -sin], 1).astype(np.float32)
    q, k = np.arange(P)[:, None] % GRID, np.arange(GRID)[None, :]
    start = np.clip(q - WIN_W // 2, 0, GRID - WIN_W)
    mask = np.where((k >= start) & (k < start + WIN_W), 0.0, MASKED).astype(np.float32)
    before = np.triu(np.ones((P, P), np.float32), 1)
    count = np.tile(np.arange(S, dtype=np.float32), (P, 1))
    return {"dft": dft, "mask": mask, "ident": np.eye(P, dtype=np.float32), "before": before, "count": count}


def kernel(**inputs):
    import concourse.bacc as bacc
    from concourse.bass_utils import run_bass_kernel_spmd

    nc = bacc.Bacc("TRN2", target_bir_lowering=False, num_devices=1, dynamic_dma_scratch_size=8192)
    arrays, args = {}, []
    slide = np.zeros((2, HEADS, SHIFTS, SLIDE), np.float32)
    for half in range(2):
        d0 = WIN_H_MAX - 1 - (ROWS - 2) - half
        slide[half, :, :, GRID - WIN_W:GRID - WIN_W + RPB_W] = inputs["nat_rpb"][0][:, d0:d0 + SHIFTS, ::-1]
    slide = slide.reshape(2, HEADS * SHIFTS, SLIDE)
    gains = np.stack([inputs["norm_mix"], inputs["norm_ffn"]], 1).reshape(4, KD, P).transpose(2, 0, 1)
    for name, a in [(n, inputs[n]) for n in _INS] + [("gains", gains), ("slide", slide)] + list(shape_constants().items()):
        a = np.ascontiguousarray(a)
        arrays[f"in_{name}"] = a
        args.append(nc.dram_tensor(f"in_{name}", a.shape, mybir.dt.from_np(a.dtype), kind="ExternalInput").ap())
    for i, (shape, dtype) in enumerate(_OUTS):
        args.append(nc.dram_tensor(f"out_{i}", shape, mybir.dt.from_np(np.dtype(dtype)), kind="ExternalOutput").ap())
    trunk(nc, *args)
    r = run_bass_kernel_spmd(nc, [arrays], core_ids=[0])
    return r.results[0]["out_0"]
```
